# Optimizing a Trainium2 kernel written in Bass

```python
import math
import jax
import jax.numpy as jnp
from jax import lax
import numpy as np

D_MODEL = 1024
BATCH = 1
SEQ = 256
DEPTH = 2

CTX_LEN = 256
GRID_W = 64
N_MIXERS = 2
N_MOD = 9
D_FF = 2816
S5_GROUP = 16
S5_GROUPS = D_MODEL // S5_GROUP
S5_STATE = 64
GDN_HEADS = 8
GDN_DK = D_MODEL // GDN_HEADS
GDN_DV = D_MODEL // GDN_HEADS
GDN_CONV = 5
GDN_CHUNK = 64
EPS = 1e-6
N_LAYERS_A = (DEPTH + 1) // 2
N_LAYERS_B = DEPTH // 2

kernel_name = "hybrid_s5_gdn_macaron_prefix_dit"

def rms_norm(x, g):
    xf = x.astype(jnp.float32)
    return xf * lax.rsqrt(jnp.mean(xf * xf, axis=-1, keepdims=True) + EPS) * g.astype(jnp.float32)

def ada_norm(x, g, shift, scale):
    return rms_norm(x, g) * (1.0 + scale) + shift

def swiglu(h, w13, w2):
    a, b = jnp.split(h @ w13, 2, axis=-1)
    return (jax.nn.silu(a) * b) @ w2

def to_col_major(h, rows):
    b, n, d = h.shape
    return h.reshape(b, rows, GRID_W, d).transpose(0, 2, 1, 3).reshape(b, n, d)

def to_row_major(h, rows):
    b, n, d = h.shape
    return h.reshape(b, GRID_W, rows, d).transpose(0, 2, 1, 3).reshape(b, n, d)

def cmul(ar, ai, br, bi):
    return ar * br - ai * bi, ar * bi + ai * br

def s5_combine(e1, e2):
    a1r, a1i, b1r, b1i = e1
    a2r, a2i, b2r, b2i = e2
    ar, ai = cmul(a2r, a2i, a1r, a1i)
    br, bi = cmul(a2r, a2i, b1r, b1i)
    return ar, ai, br + b2r, bi + b2i

def s5_states(u, a_re, a_im, log_dt, b_re, b_im):
    f32 = jnp.float32
    a_re = a_re.astype(f32)
    a_im = a_im.astype(f32)
    dt = jnp.exp(log_dt.astype(f32))[:, None]
    mag = jnp.exp(dt * a_re)
    ang = dt * a_im
    abar_re, abar_im = mag * jnp.cos(ang), mag * jnp.sin(ang)
    den = a_re * a_re + a_im * a_im
    n_re = abar_re - 1.0
    f_re = (n_re * a_re + abar_im * a_im) / den
    f_im = (abar_im * a_re - n_re * a_im) / den
    bu_re = jnp.einsum('btgc,gpc->btgp', u, b_re.astype(f32))
    bu_im = jnp.einsum('btgc,gpc->btgp', u, b_im.astype(f32))
    x_re, x_im = cmul(f_re, f_im, bu_re, bu_im)
    a_shape = (1, u.shape[1]) + abar_re.shape
    _, _, h_re, h_im = lax.associative_scan(
        s5_combine,
        (jnp.broadcast_to(abar_re, a_shape), jnp.broadcast_to(abar_im, a_shape), x_re, x_im),
        axis=1)
    return h_re, h_im

def s5_mixer(hx, hc, a_re, a_im, log_dt, b_re, b_im, c_re, c_im, d, glu_w, glu_b, with_ctx):
    bsz, seq_len, _ = hx.shape
    ctx_len = hc.shape[1]
    ux = hx.reshape(bsz, seq_len, S5_GROUPS, S5_GROUP)
    uc = hc.reshape(bsz, ctx_len, S5_GROUPS, S5_GROUP)
    yx = d * hx
    yc = d * hc
    for di in range(2):
        if di == 0:
            u = jnp.concatenate([uc, ux], axis=1)
        else:
            u = jnp.concatenate([jnp.flip(uc, 1), jnp.flip(ux, 1)], axis=1)
        h_re, h_im = s5_states(u, a_re[di], a_im[di], log_dt[di], b_re[di], b_im[di])

        def readout(hr, hi):
            y = (jnp.einsum('btgp,gcp->btgc', hr, c_re[di].astype(jnp.float32))
                 - jnp.einsum('btgp,gcp->btgc', hi, c_im[di].astype(jnp.float32)))
            y = y.reshape(bsz, -1, D_MODEL)
            return jnp.flip(y, 1) if di == 1 else y

        yx = yx + readout(h_re[:, ctx_len:], h_im[:, ctx_len:])
        if with_ctx:
            yc = yc + readout(h_re[:, :ctx_len], h_im[:, :ctx_len])

    def glu(y):
        z = jax.nn.gelu(y)
        p = z @ glu_w + glu_b
        return p[..., :D_MODEL] * jax.nn.sigmoid(p[..., D_MODEL:])

    return glu(yx), (glu(yc) if with_ctx else None)

def short_conv(u, w):
    pad = GDN_CONV // 2
    return lax.conv_general_dilated(
        u, w[:, None, :].astype(u.dtype), window_strides=(1,), padding=[(pad, pad)],
        dimension_numbers=('NWC', 'WIO', 'NWC'), feature_group_count=u.shape[-1])

def l2_normalise(t):
    tf = t.astype(jnp.float32)
    return tf * lax.rsqrt(jnp.sum(tf * tf, axis=-1, keepdims=True) + EPS)

def gdn_branch(p, conv_w, a_log, dt_bias):
    f32 = jnp.float32
    b, n, _ = p.shape
    qkv = jax.nn.silu(short_conv(p[..., :3 * D_MODEL], conv_w))
    q = l2_normalise(qkv[..., :D_MODEL].reshape(b, n, GDN_HEADS, GDN_DK)) * (GDN_DK ** -0.5)
    k = l2_normalise(qkv[..., D_MODEL:2 * D_MODEL].reshape(b, n, GDN_HEADS, GDN_DK))
    v = qkv[..., 2 * D_MODEL:].reshape(b, n, GDN_HEADS, GDN_DV).astype(f32)
    z = p[..., 3 * D_MODEL:4 * D_MODEL]
    o0 = 4 * D_MODEL
    beta = jax.nn.sigmoid(p[..., o0:o0 + 2 * GDN_HEADS].astype(f32)).reshape(b, n, 2, GDN_HEADS)
    alpha = p[..., o0 + 2 * GDN_HEADS:].astype(f32).reshape(b, n, 2, GDN_HEADS)
    g = -jnp.exp(a_log.astype(f32)) * jax.nn.softplus(alpha + dt_bias.astype(f32))
    return q, k, v, z, beta, g

def gated_delta_chunked(q, k, v, g, beta):
    bsz, n_pos, nh, dk = q.shape
    dv = v.shape[-1]
    nc = n_pos // GDN_CHUNK

    def chunks(t):
        return t.reshape(bsz, nc, GDN_CHUNK, nh, -1).transpose(0, 3, 1, 2, 4)

    q, k, v = chunks(q), chunks(k), chunks(v)
    g = g.reshape(bsz, nc, GDN_CHUNK, nh).transpose(0, 3, 1, 2)
    beta = beta.reshape(bsz, nc, GDN_CHUNK, nh).transpose(0, 3, 1, 2)
    gcum = jnp.cumsum(g, axis=-1)
    incl = jnp.tril(jnp.ones((GDN_CHUNK, GDN_CHUNK), dtype=bool))
    strict = jnp.tril(jnp.ones((GDN_CHUNK, GDN_CHUNK), dtype=bool), k=-1)
    decay = jnp.exp(jnp.where(incl, gcum[..., :, None] - gcum[..., None, :], -jnp.inf))
    k_beta = k * beta[..., None]
    a_mat = jnp.where(strict, jnp.einsum('bhncd,bhnsd->bhncs', k_beta, k) * decay, 0.0)
    lhs = a_mat + jnp.eye(GDN_CHUNK, dtype=a_mat.dtype)
    u_val = lax.linalg.triangular_solve(lhs, v * beta[..., None], left_side=True, lower=True)
    w_key = lax.linalg.triangular_solve(lhs, k_beta * jnp.exp(gcum)[..., None], left_side=True, lower=True)
    attn = jnp.where(incl, jnp.einsum('bhncd,bhnsd->bhncs', q, k) * decay, 0.0)
    q_dec = q * jnp.exp(gcum)[..., None]
    k_dec = k * jnp.exp(gcum[..., -1:] - gcum)[..., None]
    g_last = jnp.exp(gcum[..., -1])

    def step(state, inp):
        qd, kd, uv, wk, at, gl = inp
        v_new = uv - jnp.einsum('bhcd,bhde->bhce', wk, state)
        o = jnp.einsum('bhcd,bhde->bhce', qd, state) + jnp.einsum('bhcs,bhse->bhce', at, v_new)
        state = state * gl[..., None, None] + jnp.einsum('bhcd,bhce->bhde', kd, v_new)
        return state, o

    xs = tuple(jnp.moveaxis(t, 2, 0) for t in (q_dec, k_dec, u_val, w_key, attn, g_last))
    s0 = jnp.zeros((bsz, nh, dk, dv), jnp.float32)
    _, o = lax.scan(step, s0, xs)
    return o.transpose(1, 0, 3, 2, 4).reshape(bsz, n_pos, nh, dv)

def gdn_mixer(hx, hc, rows, w_in, conv_w, a_log, dt_bias, norm_g, w_out, with_ctx):
    ctx_len = hc.shape[1]
    qx, kx, vx, zx, bx, gx = gdn_branch(to_col_major(hx, rows) @ w_in, conv_w, a_log, dt_bias)
    qc, kc, vc, zc, bc, gc = gdn_branch(hc @ w_in, conv_w, a_log, dt_bias)
    ox, oc = None, None
    for di in range(2):
        def cat(tc, tx):
            if di == 0:
                return jnp.concatenate([tc, tx], axis=1)
            return jnp.concatenate([jnp.flip(tc, 1), jnp.flip(tx, 1)], axis=1)

        o = gated_delta_chunked(cat(qc, qx), cat(kc, kx), cat(vc, vx),
                                cat(gc[:, :, di], gx[:, :, di]), cat(bc[:, :, di], bx[:, :, di]))
        o_c, o_x = o[:, :ctx_len], o[:, ctx_len:]
        if di == 1:
            o_c, o_x = jnp.flip(o_c, 1), jnp.flip(o_x, 1)
        ox = o_x if ox is None else ox + o_x
        if with_ctx:
            oc = o_c if oc is None else oc + o_c

    def project(o, z):
        b, n = o.shape[:2]
        y = rms_norm(o, norm_g) * jax.nn.silu(z.reshape(b, n, GDN_HEADS, GDN_DV))
        return y.reshape(b, n, D_MODEL) @ w_out

    yx = to_row_major(project(ox, zx), rows)
    yc = project(oc, zc) if with_ctx else None
    return yx, yc

def setup_inputs(seed: int = 0) -> dict:
    key = jax.random.key(seed)
    ks = jax.random.split(key, 32)
    f32 = jnp.float32
    H = GDN_HEADS

    def nrm(k, shape, scale):
        return jax.random.normal(k, shape, f32) * scale

    x = nrm(ks[0], (BATCH, SEQ, D_MODEL), 1.0)
    c = nrm(ks[1], (BATCH, D_MODEL), 1.0)
    ctx = nrm(ks[2], (BATCH, CTX_LEN, D_MODEL), 1.0)
    c_ctx = nrm(ks[3], (D_MODEL,), 1.0)
    mod_w = nrm(ks[4], (DEPTH, D_MODEL, N_MOD * D_MODEL), 0.5 * D_MODEL ** -0.5)
    mod_b = nrm(ks[5], (DEPTH, N_MOD * D_MODEL), 0.01)
    norm_g = 1.0 + nrm(ks[6], (DEPTH, 3, D_MODEL), 0.01)
    ffn_w13 = nrm(ks[7], (DEPTH, 2, D_MODEL, 2 * D_FF), D_MODEL ** -0.5)
    ffn_w2 = nrm(ks[8], (DEPTH, 2, D_FF, D_MODEL), D_FF ** -0.5)
    na = N_LAYERS_A
    s5_a_re = -0.5 + nrm(ks[9], (na, 2, S5_GROUPS, S5_STATE), 0.01)
    s5_a_im = jnp.pi * jnp.arange(S5_STATE, dtype=f32) + nrm(ks[10], (na, 2, S5_GROUPS, S5_STATE), 0.01)
    s5_log_dt = jax.random.uniform(ks[11], (na, 2, S5_GROUPS), f32, math.log(1e-3), math.log(1e-1))
    s5_b_re = nrm(ks[12], (na, 2, S5_GROUPS, S5_STATE, S5_GROUP), (2 * S5_GROUP) ** -0.5)
    s5_b_im = nrm(ks[13], (na, 2, S5_GROUPS, S5_STATE, S5_GROUP), (2 * S5_GROUP) ** -0.5)
    s5_c_re = nrm(ks[14], (na, 2, S5_GROUPS, S5_GROUP, S5_STATE), S5_STATE ** -0.5)
    s5_c_im = nrm(ks[15], (na, 2, S5_GROUPS, S5_GROUP, S5_STATE), S5_STATE ** -0.5)
    s5_d = nrm(ks[16], (na, D_MODEL), 1.0)
    s5_glu_w = nrm(ks[17], (na, D_MODEL, 2 * D_MODEL), D_MODEL ** -0.5)
    s5_glu_b = nrm(ks[18], (na, 2 * D_MODEL), 0.01)
    nb = N_LAYERS_B
    gdn_w_in = nrm(ks[19], (nb, D_MODEL, 4 * D_MODEL + 4 * H), D_MODEL ** -0.5)
    gdn_conv_w = nrm(ks[20], (nb, GDN_CONV, 3 * D_MODEL), GDN_CONV ** -0.5)
    gdn_a_log = jnp.log(jax.random.uniform(ks[21], (nb, 2, H), f32, 1.0, 16.0))
    dt = jnp.exp(jax.random.uniform(ks[22], (nb, 2, H), f32, math.log(1e-3), math.log(1e-1)))
    gdn_dt_bias = dt + jnp.log(-jnp.expm1(-dt))
    gdn_norm_g = 1.0 + nrm(ks[23], (nb, GDN_DV), 0.01)
    gdn_w_out = nrm(ks[24], (nb, D_MODEL, D_MODEL), D_MODEL ** -0.5)
    final_g = 1.0 + nrm(ks[25], (D_MODEL,), 0.01)
    return {"x": x, "c": c, "ctx": ctx, "c_ctx": c_ctx,
            "mod_w": mod_w, "mod_b": mod_b, "norm_g": norm_g,
            "ffn_w13": ffn_w13, "ffn_w2": ffn_w2,
            "s5_a_re": s5_a_re, "s5_a_im": s5_a_im, "s5_log_dt": s5_log_dt,
            "s5_b_re": s5_b_re, "s5_b_im": s5_b_im, "s5_c_re": s5_c_re, "s5_c_im": s5_c_im,
            "s5_d": s5_d, "s5_glu_w": s5_glu_w, "s5_glu_b": s5_glu_b,
            "gdn_w_in": gdn_w_in, "gdn_conv_w": gdn_conv_w, "gdn_a_log": gdn_a_log,
            "gdn_dt_bias": gdn_dt_bias, "gdn_norm_g": gdn_norm_g, "gdn_w_out": gdn_w_out,
            "final_g": final_g}

def reference(x, c, ctx, c_ctx, mod_w, mod_b, norm_g, ffn_w13, ffn_w2,
              s5_a_re, s5_a_im, s5_log_dt, s5_b_re, s5_b_im, s5_c_re, s5_c_im,
              s5_d, s5_glu_w, s5_glu_b,
              gdn_w_in, gdn_conv_w, gdn_a_log, gdn_dt_bias, gdn_norm_g, gdn_w_out,
              final_g):
    bsz, seq_len, _ = x.shape
    rows = seq_len // GRID_W
    cx = ctx
    for i in range(DEPTH):
        last = i == DEPTH - 1
        mx = (jax.nn.silu(c) @ mod_w[i] + mod_b[i]).reshape(bsz, N_MOD, 1, D_MODEL)
        mc = (jax.nn.silu(c_ctx) @ mod_w[i] + mod_b[i]).reshape(N_MOD, 1, 1, D_MODEL)
        x = x + 0.5 * mx[:, 2] * swiglu(ada_norm(x, norm_g[i, 0], mx[:, 0], mx[:, 1]), ffn_w13[i, 0], ffn_w2[i, 0])
        cx = cx + 0.5 * mc[2] * swiglu(ada_norm(cx, norm_g[i, 0], mc[0], mc[1]), ffn_w13[i, 0], ffn_w2[i, 0])
        hx = ada_norm(x, norm_g[i, 1], mx[:, 3], mx[:, 4])
        hc = ada_norm(cx, norm_g[i, 1], mc[3], mc[4])
        j = i // N_MIXERS
        if i % N_MIXERS == 0:
            ox, oc = s5_mixer(hx, hc, s5_a_re[j], s5_a_im[j], s5_log_dt[j], s5_b_re[j], s5_b_im[j],
                              s5_c_re[j], s5_c_im[j], s5_d[j], s5_glu_w[j], s5_glu_b[j], not last)
        else:
            ox, oc = gdn_mixer(hx, hc, rows, gdn_w_in[j], gdn_conv_w[j], gdn_a_log[j], gdn_dt_bias[j],
                               gdn_norm_g[j], gdn_w_out[j], not last)
        x = x + mx[:, 5] * ox
        x = x + 0.5 * mx[:, 8] * swiglu(ada_norm(x, norm_g[i, 2], mx[:, 6], mx[:, 7]), ffn_w13[i, 1], ffn_w2[i, 1])
        if not last:
            cx = cx + mc[5] * oc
            cx = cx + 0.5 * mc[8] * swiglu(ada_norm(cx, norm_g[i, 2], mc[6], mc[7]), ffn_w13[i, 1], ffn_w2[i, 1])
    return rms_norm(x, final_g)


_drawn_inputs = setup_inputs


def setup_inputs(seed=0):
    import zlib

    import numpy as np

    out = dict(_drawn_inputs(seed))
    spreads = {}
    factors = {'mod_b': 4.577,
     'norm_g': 8.0,
     's5_a_re': 64.0,
     's5_a_im': 15.986,
     's5_log_dt': 19.557,
     's5_b_re': 32.902,
     's5_b_im': 31.227,
     's5_c_re': 32.717,
     's5_c_im': 32.636,
     's5_glu_b': 64.0,
     'gdn_norm_g': 54.344,
     'final_g': 31.551}
    for name, (base, spread) in spreads.items():
        noise = np.random.default_rng([zlib.crc32(name.encode()), seed]).standard_normal(out[name].shape)
        drawn = base * np.exp(spread * noise) if base else spread * noise
        out[name] = jnp.asarray(drawn.astype(out[name].dtype))
    for name, factor in factors.items():
        out[name] = (out[name] * factor).astype(out[name].dtype)
    return out
```

```python
from contextlib import ExitStack

import numpy as np

import concourse.bass as bass
from concourse import mybir

F32 = mybir.dt.float32
F32R = mybir.dt.float32r
ACT = mybir.ActivationFunctionType
ALU = mybir.AluOpType

P = 128
D = 1024
KT = D // P
CTX = 256
LAT = 256
T = CTX + LAT
FF = 2816
FT = FF // P
FH = FT // 2
NMOD = 9
EPS = 1e-6
GRID_W = 64
ROWS = LAT // GRID_W
BLK = 2048

G = 64
PR = G // 2
C16 = 16
L = 8
NK = T // L
KC = CTX // L
GPB = 4
NB5 = PR // GPB
ZW = 2 * L - 1

H = 8
CH = 128
NCH = T // CH

PHASES = [("f0a", FT, BLK), ("f0b", 2 * KT, FH * P), ("glu", KT, BLK), ("f1a", FT, BLK), ("f1b", 2 * KT, FH * P),
          ("f2a", FT, BLK), ("f2b", 2 * KT, FH * P), ("gdn", 2 * H, BLK), ("wo", KT // 2, BLK),
          ("f3a", FT, BLK), ("f3b", 2 * KT, FH * P)]
BASE = {}
_at = 0
for _n, _b, _c in PHASES:
    BASE[_n] = _at
    _at += _b
BLOCKS = _at
COUNT = {n: b for n, b, _ in PHASES}
COLS = {n: c for n, _, c in PHASES}

MS = 4
MB = NMOD * KT // 2

CONSTS = ["mean", "one", "eye", "tri0", "tri1", "strict0", "strict1", "bd16", "e32", "e64", "e128", "m16"]

NORMS = [(0, 0, 0, "ffn"), (0, 1, 0, "s5"), (0, 2, 0, "ffn"), (1, 0, 0, "ffn"), (1, 1, 0, "gdn"), (1, 2, CTX, "ffn")]
NORM_OF_FFN = [0, 2, 3, 5]
X_STAGE_OF_FFN = [0, 2, 3, 5]
PIECES = [(2 if c0 == 0 else 1) * KT for _, _, c0, _ in NORMS]


def pieces_before(m, of=("ffn", "s5", "gdn")):
    return sum(p for p, (_, _, _, k) in zip(PIECES[:m], NORMS[:m]) if k in of)

TWO_PI = [6.28125, 0.0019350051879882812, 3.01991598196e-07]
PREP_ANGLE = 8
GATE_G = 10


def program(nc, A, out):
    ctx = ExitStack()
    with ctx:
        def sem(name):
            return ctx.enter_context(nc.semaphore(name))

        def pair(name):
            return [sem(f"{name}{i}") for i in range(2)]

        def sb(name, shape, dt=F32, stack=None):
            return (stack or ctx).enter_context(nc.sbuf_tensor(name, shape, dt))

        x = sb("x", [P, KT, T])
        raw = sb("raw", [P, 2, BLK])
        whi = sb("whi", [P, 2, BLK], F32R)
        wlo = sb("wlo", [P, 2, BLK], F32R)
        consts = sb("consts", [P, len(CONSTS), P])
        mods = sb("mods", [P, 2, NMOD * KT, 2])
        gs = sb("gs", [P, 2, 3, KT, 2])
        hg = sb("hg", [P, 2, 3, KT, 2])
        ng = sb("ng", [P, 2, 3, KT])
        fg = sb("fg", [P, KT])
        rstd = sb("rstd", [P, T])
        std = sb("std", [P, T])
        epst = sb("epst", [P, 1])
        glub = sb("glub", [P, 2, KT])
        modb = sb("modb", [P, 2, NMOD * KT])
        gwa = sb("gwa", [P, KT, 4 * H])
        gwah = sb("gwah", [P, KT, 4 * H], F32R)
        gwal = sb("gwal", [P, KT, 4 * H], F32R)
        cvec = sb("cvec", [P, KT, 2])
        PS = ctx.enter_context(nc.psum_tensor("PS", [P, 8, 512], F32))

        def const(name):
            return consts[:, CONSTS.index(name), :]

        ffn = ExitStack()
        hidh = sb("hidh", [P, FT, T], F32R, ffn)
        hidl = sb("hidl", [P, FT, T], F32R, ffn)
        sil = sb("sil", [P, 2, T], F32, ffn)
        gt = sb("gt", [P, 2, T], F32, ffn)
        hh = sb("hh", [P, KT, T], F32R, ffn)
        hl = sb("hl", [P, KT, T], F32R, ffn)
        ffn.close()
        pre = ExitStack()
        modw = sb("modw", [P, MS, KT, 256], F32, pre)
        pre.close()
        nrm = ExitStack()
        tmp = sb("tmp", [P, KT, T], F32, nrm)
        nrm.close()

        par_in = sem("par_in")
        NPAR = 6
        mod_in = [sem(f"mod_in{s}") for s in range(MS)]
        mod_used = [sem(f"mod_used{s}") for s in range(MS)]
        silu_c = sem("silu_c")
        mods_ready = sem("mods_ready")
        raw_in = pair("raw_in")
        whi_ready = pair("whi_ready")
        wlo_ready = pair("wlo_ready")
        blk_done = pair("blk_done")
        sq_ready = sem("sq_ready")
        ss_ready = sem("ss_ready")
        std_ready = sem("std_ready")
        rstd_ready = sem("rstd_ready")
        nt_ready = sem("nt_ready")
        hh_ready = sem("hh_ready")
        norm_done = sem("norm_done")
        ab_free = pair("ab_free")
        sil_ready = pair("sil_ready")
        gt_ready = pair("gt_ready")
        hidh_ready = pair("hidh_ready")
        hid_ready = pair("hid_ready")
        x_ready = pair("x_ready")
        out_done = sem("out_done")
        fin_ready = sem("fin_ready")

        def mm3(pe, dst, slot, c, xh, xl, first, last):
            w_h, w_l = whi[:, slot, c:c + P], wlo[:, slot, c:c + P]
            pe.matmul(dst, w_h, xh, start=first, stop=False)
            pe.matmul(dst, w_h, xl, start=False, stop=False)
            return pe.matmul(dst, w_l, xh, start=False, stop=last)

        def load_blocks(sp, name, first=0, end=None):
            with sp.Fori(first, COUNT[name] // 2 if end is None else end) as i:
                for s in range(2):
                    use = BASE[name] // 2 + i
                    sp.wait_ge(wlo_ready[s], 1 + use)
                    sp.dma_start(raw[:, s, 0:COLS[name]], A["w_" + name][bass.ds(2 * i + s, 1)].rearrange("a p n -> (a p) n"))\
                        .then_inc(raw_in[s], 16)

        def split_hi(act, s, use):
            act.wait_ge(raw_in[s], 16 * use + 16)
            act.wait_ge(blk_done[s], 1 + use)
            act.activation(whi[:, s, :], raw[:, s, :], ACT.Copy).then_inc(whi_ready[s], 1)

        def split_lo(dve, s, use):
            dve.wait_ge(whi_ready[s], use + 1)
            dve.tensor_tensor(wlo[:, s, :], raw[:, s, :], whi[:, s, :].bitcast(F32), ALU.subtract)\
                .then_inc(wlo_ready[s], 1)

        def blocks(eng, name, split, work, start=0):
            n, u0 = COUNT[name] // 2, BASE[name] // 2
            whole = n - (BASE[name] + COUNT[name] == BLOCKS)
            with eng.Fori(0, whole) as i:
                split(eng, 1, u0 + i)
                work(i, 0)
                split(eng, 0, u0 + i + 1)
                work(i, 1)
            if whole < n:
                split(eng, 1, u0 + n - 1)
                work(n - 1, 0)
                work(n - 1, 1)

        def halves(c0):
            return [w for w in range(2) if w * CTX >= c0]

        def cols(w):
            return slice(CTX * w, CTX * w + CTX)

        def part(t, k, w, turned):
            v = t[:, bass.ds(k, 1), cols(w)]
            if w and turned:
                return v.rearrange("p a (c r) -> p (a r) c", r=ROWS)
            return v.rearrange("p a (r c) -> p (a r) c", r=ROWS)

        def s5_part(k, w):
            return hS[:, bass.ds(k, 1), :, KC * w:KC * w + KC].rearrange("p a s k -> p (a s) k")

        def natural_sk(t, k, w):
            return t[:, bass.ds(k, 1), cols(w)].rearrange("p a (k s) -> p (a s) k", s=L)

        def norm_act(act, m):
            layer, n, c0, feeds = NORMS[m] if m < len(NORMS) else (0, 0, CTX, "out")
            if m:
                for q in range(2):
                    act.wait_ge(x_ready[q], 1 + KT // 2 * m)
            else:
                act.wait_ge(mods_ready, 4)
            with act.Fori(0, KT) as k:
                act.activation(tmp[:, bass.ds(k, 1), c0:T], x[:, bass.ds(k, 1), c0:T], ACT.Square).then_inc(sq_ready, 1)
            act.wait_ge(ss_ready, m + 1)
            act.activation(std[:, c0:T], PS[:, 6, c0:T], ACT.Sqrt, bias=epst[:, 0:1]).then_inc(std_ready, 1)
            if feeds == "out":
                return
            b = pieces_before(m)
            with act.Fori(0, KT) as k:
                for j, w in enumerate(halves(c0)):
                    act.wait_ge(nt_ready, b + len(halves(c0)) * k + j + 1)
                    shift = mods[:, layer, bass.ds(3 * n * KT + k, 1), w:w + 1].rearrange("p a b -> p (a b)")
                    if feeds == "s5":
                        act.activation(s5_part(k, w), natural_sk(tmp, k, w), ACT.Identity, bias=shift).then_inc(hh_ready, 1)
                    else:
                        act.activation(part(hh, k, w, feeds == "gdn"), part(tmp, k, w, False), ACT.Identity,
                                       bias=shift).then_inc(hh_ready, 1)

        def norm_pe(pe, m):
            c0 = NORMS[m][2] if m < len(NORMS) else CTX
            for k in range(KT):
                pe.wait_ge(sq_ready, KT * m + k + 1)
                last = pe.matmul(PS[:, 6, c0:T], const("mean"), tmp[:, k, c0:T], start=k == 0, stop=k == KT - 1)
            last.then_inc(ss_ready, 1)

        def norm_dve(dve, m):
            layer, n, c0, feeds = NORMS[m]
            hs = halves(c0)
            dve.wait_ge(std_ready, m + 1)
            dve.reciprocal(rstd[:, c0:T], std[:, c0:T]).then_inc(rstd_ready, 1)
            dve.wait_ge(rstd_ready, m + 1)
            if m == 0:
                dve.wait_ge(mods_ready, 4)
            with dve.Fori(0, KT) as k:
                for w in hs:
                    dve.scalar_tensor_tensor(
                        out=tmp[:, bass.ds(k, 1), cols(w)].rearrange("p a t -> p (a t)"),
                        in0=x[:, bass.ds(k, 1), cols(w)].rearrange("p a t -> p (a t)"),
                        scalar=gs[:, layer, n, bass.ds(k, 1), w:w + 1].rearrange("p a b -> p (a b)"),
                        in1=rstd[:, cols(w)], op0=ALU.mult, op1=ALU.mult).then_inc(nt_ready, 1)
            if feeds == "s5":
                return
            b = pieces_before(m)
            with dve.Fori(0, KT) as k:
                for j, w in enumerate(hs):
                    dve.wait_ge(hh_ready, b + len(hs) * k + j + 1)
                    dve.wait_ge(nt_ready, b + len(hs) * k + j + 1)
                    turned = feeds == "gdn"
                    dve.scalar_tensor_tensor(
                        out=part(hl, k, w, turned), in0=part(tmp, k, w, False),
                        scalar=mods[:, layer, bass.ds(3 * n * KT + k, 1), w:w + 1].rearrange("p a b -> p (a b)"),
                        in1=part(hh, k, w, turned).bitcast(F32), op0=ALU.add, op1=ALU.subtract).then_inc(norm_done, 1)

        def final_dve(dve):
            m = len(NORMS)
            dve.wait_ge(std_ready, m + 1)
            dve.reciprocal(rstd[:, CTX:T], std[:, CTX:T]).then_inc(rstd_ready, 1)
            dve.wait_ge(rstd_ready, m + 1)
            with dve.Fori(0, KT) as k:
                dve.scalar_tensor_tensor(
                    out=tmp[:, bass.ds(k, 1), CTX:T].rearrange("p a t -> p (a t)"),
                    in0=x[:, bass.ds(k, 1), CTX:T].rearrange("p a t -> p (a t)"), scalar=fg[:, bass.ds(k, 1)],
                    in1=rstd[:, CTX:T], op0=ALU.mult, op1=ALU.mult).then_inc(fin_ready, 1)

        def ffn_pe(pe, f):
            a, b, c0 = f"f{f}a", f"f{f}b", NORMS[NORM_OF_FFN[f]][2]
            pe.wait_ge(norm_done, pieces_before(NORM_OF_FFN[f] + 1, ("ffn", "gdn")))
            with pe.Fori(0, FT // 2) as i:
                for s in range(2):
                    pe.wait_ge(wlo_ready[s], 1 + BASE[a] // 2 + i + 1)
                    pe.wait_ge(gt_ready[s], 1 + FT // 2 * f + i)
                    for ab in range(2):
                        for k in range(KT):
                            last = mm3(pe, PS[:, 2 * ab + s, c0:T], s, (2 * k + ab) * P, hh[:, k, c0:T], hl[:, k, c0:T],
                                       k == 0, k == KT - 1)
                    last.then_inc(blk_done[s], 1)
            for s in range(2):
                pe.wait_ge(hid_ready[s], 1 + FT // 2 * (f + 1))
            with pe.Fori(0, KT // 2) as i:
                for q in range(2):
                    pe.wait_ge(x_ready[q], 1 + KT // 2 * X_STAGE_OF_FFN[f] + i)
                    for s in range(2):
                        pe.wait_ge(wlo_ready[s], 1 + BASE[b] // 2 + 2 * i + q + 1)
                        for k in range(FH):
                            last = mm3(pe, PS[:, 4 + q, c0:T], s, k * P, hidh[:, FH * s + k, c0:T], hidl[:, FH * s + k, c0:T],
                                       s == 0 and k == 0, s == 1 and k == FH - 1)
                        last.then_inc(blk_done[s], 1)

        def ffn_act(act, f):
            a, b, c0 = f"f{f}a", f"f{f}b", NORMS[NORM_OF_FFN[f]][2]

            def silu(i, s):
                act.wait_ge(blk_done[s], 1 + BASE[a] // 2 + i + 1)
                act.activation(sil[:, s, c0:T], PS[:, s, c0:T], ACT.Silu).then_inc(sil_ready[s], 1)

            blocks(act, a, split_hi, silu)
            blocks(act, b, split_hi, lambda i, s: None)

        def ffn_dve(dve, f):
            a, b, c0 = f"f{f}a", f"f{f}b", NORMS[NORM_OF_FFN[f]][2]
            layer, n = NORMS[NORM_OF_FFN[f]][0:2]

            def gate(i, s):
                dve.wait_ge(sil_ready[s], FT // 2 * f + i + 1)
                dve.wait_ge(hid_ready[s], 1 + FT // 2 * f + i)
                dve.tensor_tensor(gt[:, s, c0:T], sil[:, s, c0:T], PS[:, 2 + s, c0:T], ALU.mult).then_inc(gt_ready[s], 1)

            blocks(dve, a, split_lo, gate)
            u0 = BASE[b] // 2

            def update(i, last_block):
                for q in range(2):
                    split_lo(dve, 1, u0 + 2 * i + q)
                    if not (last_block and q == 1):
                        split_lo(dve, 0, u0 + 2 * i + q + 1)
                    dve.wait_ge(blk_done[1], 1 + u0 + 2 * i + q + 1)
                    add_to_x(dve, layer, n, 2 * i + q, c0, 4 + q, None).then_inc(x_ready[q], 1)

            ends = BASE[b] + COUNT[b] == BLOCKS
            with dve.Fori(0, KT // 2 - ends) as i:
                update(i, False)
            if ends:
                update(KT // 2 - 1, True)

        def add_to_x(dve, layer, n, dt, c0, bank, order):
            for w in halves(c0):
                xv, pv = x[:, bass.ds(dt, 1), cols(w)], PS[:, bank, cols(w)]
                if order == "sk":
                    xv = xv.rearrange("p a (k s) -> p (a s) k", s=L)
                    pv = None
                elif order == "turned":
                    xv = xv.rearrange("p a (r c) -> p (a r) c", r=ROWS)
                    pv = PS[:, bank, 0:LAT].rearrange("p (c r) -> p r c", r=ROWS)
                else:
                    xv = xv.rearrange("p a t -> p (a t)")
                last = dve.scalar_tensor_tensor(
                    out=xv, in0=pv, scalar=hg[:, layer, n, bass.ds(dt, 1), w:w + 1].rearrange("p a b -> p (a b)"),
                    in1=xv, op0=ALU.mult, op1=ALU.add)
            return last

        def ffn_pool(pool, f):
            c0 = NORMS[NORM_OF_FFN[f]][2]
            with pool.Fori(0, FT // 2) as i:
                for s in range(2):
                    pool.wait_ge(gt_ready[s], 1 + FT // 2 * f + i + 1)
                    pool.tensor_copy(hidh[:, bass.ds(2 * i + s, 1), c0:T], gt[:, s:s + 1, c0:T]).then_inc(hidh_ready[s], 1)
                    pool.wait_ge(hidh_ready[s], FT // 2 * f + i + 1)
                    pool.tensor_tensor(hidl[:, bass.ds(2 * i + s, 1), c0:T], gt[:, s:s + 1, c0:T],
                                       hidh[:, bass.ds(2 * i + s, 1), c0:T].bitcast(F32), ALU.subtract)\
                        .then_inc(hid_ready[s], 1)

        def mods_pe(pe):
            pe.wait_ge(silu_c, 1)
            for layer in range(2):
                with pe.Fori(0, MB // MS) as i:
                    for s in range(MS):
                        pe.wait_ge(mod_in[s], 16 * (MB // MS * layer + i) + 16)
                        for h in range(2):
                            at = 4 * MS * i + 4 * s + 2 * h
                            for k in range(KT):
                                last = pe.matmul(PS[:, 4 + layer, bass.ds(at, 2)], modw[:, s, k, h * P:(h + 1) * P], cvec[:, k, :],
                                                 start=k == 0, stop=k == KT - 1)
                        last.then_inc(mod_used[s], 1)

        def mods_dve(dve):
            dve.memset(epst[:, :], EPS).then_inc(mods_ready, 1)
            dve.wait_ge(par_in, 16 * NPAR)
            for layer in range(2):
                for s in range(MS):
                    dve.wait_ge(mod_used[s], 1 + MB // MS * (layer + 1))
                dve.tensor_tensor(mods[:, layer, :, :], PS[:, 4 + layer, 0:2 * NMOD * KT].rearrange("p (a w) -> p a w", w=2),
                                  modb[:, layer, :].unsqueeze(2).to_broadcast([P, NMOD * KT, 2]), ALU.add).then_inc(mods_ready, 1)
            dve.wait_ge(mods_ready, 3)
            for layer in range(2):
                for n in range(3):
                    scale = mods[:, layer, (3 * n + 1) * KT:(3 * n + 2) * KT, :]
                    gate = mods[:, layer, (3 * n + 2) * KT:(3 * n + 3) * KT, :]
                    dve.scalar_tensor_tensor(out=gs[:, layer, n, :, :], in0=scale, scalar=1.0,
                                             in1=ng[:, layer, n, :].unsqueeze(2).to_broadcast([P, KT, 2]),
                                             op0=ALU.add, op1=ALU.mult)
                    last = dve.tensor_scalar(hg[:, layer, n, :, :], gate, 1.0 if n == 1 else 0.5, None, ALU.mult)
            last.then_inc(mods_ready, 1)
        prs = ExitStack()
        s5p = sb("s5p", [P, 3, 64], F32, prs)
        sB = sb("sB", [P, 64, 2, C16], F32, prs)
        sC = sb("sC", [P, 64, 2, C16], F32, prs)
        sd = sb("sd", [P, KT], F32, prs)
        v = sb("v", [P, 24, 64], F32, prs)
        pw = sb("pw", [P, 2, 64, L + 1], F32, prs)
        rv = sb("rv", [P, 2, 64, L + 1], F32, prs)
        cf = sb("cf", [P, 64, 2, C16], F32, prs)
        bz = sb("bz", [P, 8, 2, 2 * C16], F32, prs)
        et = sb("et", [P, 3, 64, NK], F32, prs)
        bx = sb("bx", [P, 8, 2, L, C16], F32, prs)
        cx = sb("cx", [P, 8, 2, L + 1, C16], F32, prs)
        t1 = sb("t1", [P, 64 * NK // 2], F32, prs)
        t2 = sb("t2", [P, 64 * C16], F32, prs)
        vws = sb("vws", [P, 8, 2, P], F32, prs)
        zs = sb("zs", [P, ZW, C16], F32, prs)
        prs.close()

        vwd = nc.dram_tensor("vwd", (NB5, P, 8, 2, P), F32, kind="Internal").ap()
        cxd = nc.dram_tensor("cxd", (NB5, P, 8, 2, L + 1, C16), F32, kind="Internal").ap()
        etd = nc.dram_tensor("etd", (NB5, P, 3, 8, NK), F32, kind="Internal").ap()
        zd = nc.dram_tensor("zd", (D, ZW * C16), F32, kind="Internal").ap()
        hd = nc.dram_tensor("hd", (D, T), F32, kind="Internal").ap()
        yd = nc.dram_tensor("yd", (D, T), F32, kind="Internal").ap()

        s5st = ExitStack()
        U = sb("U", [P, G, NK], F32, s5st)
        hS = sb("hS", [P, KT, L, NK], F32, s5st)
        vwS = sb("vwS", [P, 2, 8, 2, P], F32, s5st)
        cxS = sb("cxS", [P, 2, 8, 2, L + 1, C16], F32, s5st)
        etS = sb("etS", [P, 2, 3, 8, NK], F32, s5st)
        mS = sb("mS", [P, 2, 8, P], F32, s5st)
        wr = sb("wr", [P, 2, 8 * NK], F32, s5st)
        gr = sb("gr", [P, 2, 8 * NK], F32, s5st)
        ta = sb("ta", [P, 8, NK], F32, s5st)
        tb = sb("tb", [P, 8, NK], F32, s5st)
        tc = sb("tc", [P, 8, NK], F32, s5st)
        td = sb("td", [P, 8, NK], F32, s5st)
        Hs = sb("Hs", [P, 2, 2, 8, NK + 1], F32, s5st)
        Yt = sb("Yt", [P, 2, 8, NK], F32, s5st)
        s5st.close()

        s5_par = sem("s5_par")
        v_step = sem("v_step")
        v_act = sem("v_act")
        et_ready = sem("et_ready")
        et_out = sem("et_out")
        bx_ready = sem("bx_ready")
        cx_ready = sem("cx_ready")
        cx_used = sem("cx_used")
        bxT_ready = sem("bxT_ready")
        z_ready = sem("z_ready")
        vws_ready = sem("vws_ready")
        zs_ready = sem("zs_ready")
        vw_out = sem("vw_out")
        cx_out = sem("cx_out")
        z_out = sem("z_out")
        hd_out = sem("hd_out")
        u_in = sem("u_in")
        w5_in = pair("w5_in")
        V_ready = sem("V_ready")
        V_used = sem("V_used")
        r_step = sem("r_step")
        g_ready = sem("g_ready")
        q_step = sem("q_step")
        H_zero = sem("H_zero")
        H_ready = sem("H_ready")
        Y_ready = sem("Y_ready")
        Yt_ready = sem("Yt_ready")
        y_out = sem("y_out")
        y_in = sem("y_in")
        gelu_ready = sem("gelu_ready")
        zh_ready = sem("zh_ready")
        zl_ready = sem("zl_ready")
        sig_ready = pair("sig_ready")
        glu_ready = pair("glu_ready")
        glu_free = pair("glu_free")
        (DT, ER, ANG, RN, RR, SH, SN, CS, MAG, M8, AR, AI, NRE, DEN, FR, FI, E2R, E2I, E4R, E4I, E8R, E8I, VA, VB) = range(24)

        def col(i):
            return v[:, i, :]

        def prep_act(act):
            act.wait_ge(s5_par, 16 * 5)
            act.activation(col(DT), s5p[:, 2, :], ACT.Exp).then_inc(v_act, 1)
            act.wait_ge(v_step, 1)
            act.activation(col(MAG), col(ER), ACT.Exp).then_inc(v_act, 1)
            act.activation(col(M8), col(ER), ACT.Exp, scale=float(L)).then_inc(v_act, 1)
            act.wait_ge(v_step, PREP_ANGLE)
            act.activation(col(SN), col(RR), ACT.Sin).then_inc(v_act, 1)
            act.activation(col(SH), col(RR), ACT.Sin, scale=0.5).then_inc(v_act, 1)
            for b in range(NB5):
                if b:
                    act.wait_ge(vw_out, 16 * b)
                for q in range(4):
                    act.wait_ge(bxT_ready, 4 * b + q + 1)
                    act.activation(vws[:, 2 * q:2 * q + 2, :, :].rearrange("p a b c -> p (a b c)"), PS[:, q, :], ACT.Copy)\
                        .then_inc(vws_ready, 1)

        def prep_dve(dve):
            done = [0]

            def step(ins):
                done[0] += 1
                ins.then_inc(v_step, 1)
                dve.wait_ge(v_step, done[0])

            def tt(dst, a, b, op):
                step(dve.tensor_tensor(dst, a, b, op))

            def cmul(dr, di, ar, ai, br, bi, ta_, tb_, negative=False):
                tt(ta_, ar, br, ALU.mult)
                tt(tb_, ai, bi, ALU.mult)
                tt(dr, ta_, tb_, ALU.subtract)
                tt(ta_, ar, bi, ALU.mult)
                tt(tb_, ai, br, ALU.mult)
                if negative:
                    step(dve.scalar_tensor_tensor(out=di, in0=ta_, scalar=-1.0, in1=tb_, op0=ALU.mult, op1=ALU.subtract))
                else:
                    tt(di, ta_, tb_, ALU.add)

            are, aim = s5p[:, 0, :], s5p[:, 1, :]
            dve.wait_ge(s5_par, 16 * 5)
            dve.wait_ge(v_act, 1)
            tt(col(ER), are, col(DT), ALU.mult)
            tt(col(ANG), aim, col(DT), ALU.mult)
            magic = 1.5 * 2.0 ** 23
            step(dve.tensor_scalar(col(RN), col(ANG), 1.0 / (2.0 * np.pi), magic, ALU.mult, ALU.add))
            step(dve.tensor_scalar(col(RN), col(RN), magic, None, ALU.subtract))
            step(dve.scalar_tensor_tensor(out=col(RR), in0=col(RN), scalar=-TWO_PI[0], in1=col(ANG), op0=ALU.mult, op1=ALU.add))
            step(dve.scalar_tensor_tensor(out=col(RR), in0=col(RN), scalar=-TWO_PI[1], in1=col(RR), op0=ALU.mult, op1=ALU.add))
            step(dve.scalar_tensor_tensor(out=col(RR), in0=col(RN), scalar=-TWO_PI[2], in1=col(RR), op0=ALU.mult, op1=ALU.add))
            step(dve.tensor_scalar(col(RR), col(RR), 3.1415925, -3.1415925, ALU.min, ALU.max))
            assert done[0] == PREP_ANGLE
            dve.wait_ge(v_act, 5)
            tt(col(CS), col(SH), col(SH), ALU.mult)
            step(dve.tensor_scalar(col(CS), col(CS), -2.0, 1.0, ALU.mult, ALU.add))
            tt(col(AR), col(MAG), col(CS), ALU.mult)
            tt(col(AI), col(MAG), col(SN), ALU.mult)
            step(dve.tensor_scalar(col(NRE), col(AR), 1.0, None, ALU.subtract))
            tt(col(VA), are, are, ALU.mult)
            tt(col(VB), aim, aim, ALU.mult)
            tt(col(DEN), col(VA), col(VB), ALU.add)
            step(dve.reciprocal(col(DEN), col(DEN)))
            tt(col(VA), col(NRE), are, ALU.mult)
            tt(col(VB), col(AI), aim, ALU.mult)
            tt(col(FR), col(VA), col(VB), ALU.add)
            tt(col(FR), col(FR), col(DEN), ALU.mult)
            tt(col(VA), col(AI), are, ALU.mult)
            tt(col(VB), col(NRE), aim, ALU.mult)
            tt(col(FI), col(VA), col(VB), ALU.subtract)
            tt(col(FI), col(FI), col(DEN), ALU.mult)
            step(dve.memset(pw[:, 0, :, 0:1], 1.0))
            step(dve.memset(pw[:, 1, :, 0:1], 0.0))
            for r, c in ((0, AR), (1, AI)):
                step(dve.tensor_copy(pw[:, r, :, 1:2], col(c).unsqueeze(2)))
            for n in (1, 2, 4):
                by = [pw[:, r, :, n:n + 1].to_broadcast([P, 64, n]) for r in range(2)]
                ts = [t[:, 0:64 * n].rearrange("p (a b) -> p a b", b=n) for t in (t1, t2)]
                cmul(pw[:, 0, :, n + 1:2 * n + 1], pw[:, 1, :, n + 1:2 * n + 1],
                     pw[:, 0, :, 1:n + 1], pw[:, 1, :, 1:n + 1], by[0], by[1], ts[0], ts[1])
            step(dve.tensor_copy(rv[:, :, :, :].rearrange("p a b c -> p (a b) c"),
                                 pw[:, :, :, :].rearrange("p a b c -> p (a b) c")[:, :, ::-1]))
            cmul(col(E2R), col(E2I), col(CS), col(SN), col(CS), col(SN), col(VA), col(VB))
            cmul(col(E4R), col(E4I), col(E2R), col(E2I), col(E2R), col(E2I), col(VA), col(VB))
            cmul(col(E8R), col(E8I), col(E4R), col(E4I), col(E4R), col(E4I), col(VA), col(VB))
            step(dve.memset(et[:, 0, :, 0:1], 1.0))
            step(dve.memset(et[:, 1, :, 0:1], 0.0))
            n, cr, ci, nr, ni = 1, E8R, E8I, E2R, E2I
            while n < NK:
                by = [col(c).unsqueeze(2).to_broadcast([P, 64, n]) for c in (cr, ci)]
                wide = (t1[:, :], bx[:, :, :, :, :].rearrange("p a b c d -> p (a b c d)"))
                ts = [t[:, 0:64 * n].rearrange("p (a b) -> p a b", b=n) for t in wide]
                cmul(et[:, 0, :, n:2 * n], et[:, 1, :, n:2 * n], et[:, 0, :, 0:n], et[:, 1, :, 0:n], by[0], by[1], ts[0], ts[1])
                cmul(col(nr), col(ni), col(cr), col(ci), col(cr), col(ci), col(VA), col(VB))
                n, cr, ci, nr, ni = 2 * n, nr, ni, cr, ci
            step(dve.tensor_copy(et[:, 2, :, :], col(M8).unsqueeze(2).to_broadcast([P, 64, NK])))
            step(dve.memset(et[:, 2, :, 0:1], 0.0))
            dve.sem_inc(et_ready, 1)
            fb = [col(c).unsqueeze(2).to_broadcast([P, 64, C16]) for c in (FR, FI)]
            ts = [t[:, 0:64 * C16].rearrange("p (a b) -> p a b", b=C16) for t in (t1, t2)]
            cmul(cf[:, :, 0, :], cf[:, :, 1, :], sC[:, :, 0, :], sC[:, :, 1, :], fb[0], fb[1], ts[0], ts[1])
            step(dve.memset(bz[:, :, :, :], 0.0))
            for b in range(NB5):
                def of(t, r, d, lo, hi):
                    u = t[:, r, 8 * b + d:8 * b + 8:2, lo:hi]
                    return u.unsqueeze(3).to_broadcast([P, GPB, hi - lo, C16])

                def channels(t, r, d, n):
                    u = t[:, 8 * b + d:8 * b + 8:2, r, :]
                    return u.unsqueeze(2).to_broadcast([P, GPB, n, C16])

                if b:
                    dve.wait_ge(bxT_ready, 4 * b)
                    dve.wait_ge(cx_out, 16 * b)
                    dve.wait_ge(z_ready, b)
                for g2 in range(2):
                    step(dve.tensor_copy(bz[64 * g2:64 * g2 + 64, :, :, C16 * g2:C16 * g2 + C16],
                                         sB[64 * g2:64 * g2 + 64, 8 * b:8 * b + 8, :, :]))
                for d in range(2):
                    ts = [t[:, 0:GPB * P].rearrange("p (a b c) -> p a b c", a=GPB, b=L) for t in (t1, t2)]
                    src, lo = ((rv, 1), (pw, 0))[d]
                    cmul(bx[:, d::2, 0, :, :], bx[:, d::2, 1, :, :], channels(sB, 0, d, L), channels(sB, 1, d, L),
                         of(src, 0, d, lo, lo + L), of(src, 1, d, lo, lo + L), ts[0], ts[1])
                dve.sem_inc(bx_ready, 1)
                for d in range(2):
                    ts = [t[:, 0:GPB * 144].rearrange("p (a b c) -> p a b c", a=GPB, b=L + 1) for t in (t1, t2)]
                    src = (pw, rv)[d]
                    cmul(cx[:, d::2, 0, :, :], cx[:, d::2, 1, :, :], channels(cf, 0, d, L + 1), channels(cf, 1, d, L + 1),
                         of(src, 0, d, 0, L + 1), of(src, 1, d, 0, L + 1), ts[0], ts[1], negative=True)
                dve.sem_inc(cx_ready, 1)
                dve.wait_ge(z_ready, b + 1)
                if b:
                    dve.wait_ge(z_out, 16 * b)
                step(dve.tensor_copy(zs[:, :, :], PS[:, 7, 0:ZW * C16].rearrange("p (a b) -> p a b", b=C16)))
                step(dve.scalar_tensor_tensor(out=zs[:, L - 1, :], in0=const("m16")[:, 0:C16], scalar=sd[:, b:b + 1],
                                              in1=zs[:, L - 1, :], op0=ALU.mult, op1=ALU.add))
                dve.sem_inc(zs_ready, 1)

        def prep_pe(pe):
            pe.wait_ge(par_in, 16 * NPAR)
            for b in range(NB5):
                pe.wait_ge(bx_ready, b + 1)
                for q in range(4):
                    if b:
                        pe.wait_ge(vws_ready, 4 * (b - 1) + q + 1)
                    for j in range(4):
                        last = pe.transpose(PS[:, q, j * P:(j + 1) * P],
                                            bx[:, 2 * q + j // 2, j % 2, :, :].rearrange("p a b -> p (a b)"), const("eye"))
                    last.then_inc(bxT_ready, 1)
                pe.wait_ge(cx_ready, b + 1)
                if b:
                    pe.wait_ge(zs_ready, b)
                for pr in range(GPB):
                    for d in range(2):
                        for r in range(2):
                            gd = 2 * pr + d
                            lag = cx[:, gd, r, d:d + L, :].rearrange("p a b -> p (a b)")
                            at = (0 if d else (L - 1) * C16)
                            last = pe.matmul(PS[32 * pr:32 * pr + 32, 7, at:at + P], bz[:, gd, r, :], lag,
                                             start=d == 0 and r == 0, stop=True, skip_group_check=True,
                                             tile_position=(0, 32 * pr))
                last.then_inc(z_ready, 1)

        def prep_sp(sp):
            sp.wait_ge(et_ready, 1)
            sp.dma_start(etd.rearrange("b p r g k -> p r b (g k)"), et[:, :, :, :].rearrange("p r (b g) k -> p r b (g k)", b=NB5)).then_inc(et_out, 16)
            for b in range(NB5):
                sp.wait_ge(cx_ready, b + 1)
                sp.dma_start(cxd[b], cx[:, :, :, :, :]).then_inc(cx_out, 16)
                sp.wait_ge(vws_ready, 4 * b + 4)
                sp.dma_start(vwd[b], vws[:, :, :, :]).then_inc(vw_out, 16)
                sp.wait_ge(zs_ready, b + 1)
                sp.dma_start(zd[b * P:(b + 1) * P, :], zs[:, :, :].rearrange("p a b -> p (a b)")).then_inc(z_out, 16)

        def load_s5(sp, b):
            s = b % 2
            if b >= 2:
                sp.wait_ge(Y_ready, b - 1)
            sp.dma_start(vwS[:, s, :, :, :], vwd[b]).then_inc(w5_in[s], 16)
            sp.dma_start(cxS[:, s, :, :, :, :], cxd[b]).then_inc(w5_in[s], 16)
            sp.dma_start(etS[:, s, :, :, :], etd[b]).then_inc(w5_in[s], 16)
            for st in range(L):
                src = bass.AP(zd.tensor, zd.offset + b * P * ZW * C16 + (L - 1 - st) * C16,
                              [[ZW * C16, C16], [C16 * ZW * C16, 8], [1, P]])
                sp.dma_start(mS[C16 * st:C16 * st + C16, s, :, :], src).then_inc(w5_in[s], 16)

        def s5_sp(sp):
            sp.wait_ge(hh_ready, pieces_before(2))
            sp.dma_start(hd.rearrange("(k p) t -> p k t", p=P), hS[:, :, :, :].rearrange("p k s c -> p k (s c)")).then_inc(hd_out, 16)
            for s_, n in ((et_out, 1), (cx_out, NB5), (vw_out, NB5), (z_out, NB5)):
                sp.wait_ge(s_, 16 * n)
            load_s5(sp, 0)
            load_s5(sp, 1)
            sp.wait_ge(hd_out, 16)
            for st in range(L):
                src = bass.AP(hd.tensor, hd.offset + st * NK, [[T, C16], [C16 * T, G], [1, NK]])
                sp.dma_start(U[C16 * st:C16 * st + C16, :, :], src).then_inc(u_in, 16)
            for b in range(NB5):
                sp.wait_ge(Yt_ready, b + 1)
                for st in range(L):
                    dst = bass.AP(yd.tensor, yd.offset + b * P * T + st * NK, [[T, C16], [C16 * T, 8], [1, NK]])
                    sp.dma_start(dst, Yt[C16 * st:C16 * st + C16, b % 2, :, :]).then_inc(y_out, 16)
                if b + 2 < NB5:
                    load_s5(sp, b + 2)
                sp.wait_ge(y_out, 16 * L * (b + 1))
                sp.dma_start(hS[:, b, :, :], yd[b * P:(b + 1) * P, :].rearrange("p (s k) -> p s k", s=L)).then_inc(y_in, 16)

        def scan_order(t, d):
            return t if d == 0 else t.rearrange("p (a j) -> p a j", a=2)[:, :, ::-1]

        def s5_pe(pe):
            pe.wait_ge(u_in, 16 * L)
            for b in range(NB5 + 1):
                s = b % 2
                if b < NB5:
                    pe.wait_ge(w5_in[s], 16 * 11 * (b // 2 + 1))
                    if b >= 2:
                        pe.wait_ge(V_used, b - 1)
                    for gd in range(8):
                        for r in range(2):
                            for g2 in range(2):
                                g = 8 * b + 2 * (gd // 2) + g2
                                last = pe.matmul(PS[64 * g2:64 * g2 + 64, 2 * s + r, gd * NK:(gd + 1) * NK],
                                                 vwS[:, s, gd, r, 64 * g2:64 * g2 + 64], scan_order(U[:, g, :], gd % 2),
                                                 start=True, stop=True)
                    last.then_inc(V_ready, 1)
                if b:
                    c = b - 1
                    s = c % 2
                    pe.wait_ge(H_ready, c + 1)
                    if c >= 2:
                        pe.wait_ge(Yt_ready, c - 1)
                    for gl in range(8):
                        pr, g2 = gl // 2, gl % 2
                        rows = slice(64 * g2, 64 * g2 + 64)
                        dst = PS[:, 4 + 2 * s + g2, pr * NK:(pr + 1) * NK]
                        pe.matmul(dst, mS[:, s, gl, :], U[:, 8 * c + gl, :], start=True, stop=False)
                        for d in range(2):
                            for r in range(2):
                                w = cxS[rows, s, 2 * pr + d, r, 1 - d:1 - d + L, :].rearrange("p a b -> p (a b)")
                                last = pe.matmul(dst, w, scan_order(Hs[rows, s, r, 2 * pr + d, 0:NK], d),
                                                 start=False, stop=d == 1 and r == 1)
                    last.then_inc(Y_ready, 1)

        def s5_dve(dve):
            n = [0]

            def step(ins):
                n[0] += 1
                ins.then_inc(r_step, 1)
                dve.wait_ge(r_step, n[0])

            for b in range(NB5):
                s = b % 2
                dve.wait_ge(V_ready, b + 1)
                vr, vi = (PS[:, 2 * s + r, :].rearrange("p (g k) -> p g k", k=NK) for r in range(2))
                ec, es = etS[:, s, 0, :, :], etS[:, s, 1, :, :]
                mult = etS[:, s, 2, :, :].rearrange("p g k -> p (g k)")
                wre, wim = (wr[:, r, :].rearrange("p (g k) -> p g k", k=NK) for r in range(2))
                dve.tensor_tensor(ta[:, :, :], vr, ec, ALU.mult)
                step(dve.tensor_tensor(tb[:, :, :], vi, es, ALU.mult))
                step(dve.tensor_tensor(wre, ta[:, :, :], tb[:, :, :], ALU.add))
                dve.tensor_tensor(ta[:, :, :], vi, ec, ALU.mult)
                last = dve.tensor_tensor(tb[:, :, :], vr, es, ALU.mult)
                step(last)
                step(dve.tensor_tensor(wim, ta[:, :, :], tb[:, :, :], ALU.subtract))
                dve.sem_inc(V_used, 1)
                if b:
                    dve.wait_ge(q_step, 6 * b)
                for r in range(2):
                    last = dve.tensor_tensor_scan(gr[:, r, :], mult, wr[:, r, :], 0.0, ALU.mult, ALU.add)
                    last.then_inc(g_ready, 1)
            for k in range(KT):
                dve.wait_ge(zh_ready, k + 1)
                dve.tensor_tensor(hl[:, k, :], hS[:, k, :, :].rearrange("p s c -> p (s c)"), hh[:, k, :].bitcast(F32), ALU.subtract)\
                    .then_inc(zl_ready, 1)

            def glu(i, s):
                dt = 2 * i + s
                dve.wait_ge(sig_ready[s], i + 1)
                dve.scalar_tensor_tensor(out=gt[:, s, :], in0=PS[:, s, :], scalar=glub[:, 0, bass.ds(dt, 1)],
                                         in1=sil[:, s, :], op0=ALU.add, op1=ALU.mult).then_inc(glu_ready[s], 1)
                dve.wait_ge(glu_ready[s], 1 + i + 1)
                for w in range(2):
                    xv = x[:, bass.ds(dt, 1), cols(w)].rearrange("p a (k s) -> p (a s) k", s=L)
                    last = dve.scalar_tensor_tensor(
                        out=xv, in0=gt[:, s, :].rearrange("p (s k) -> p s k", s=L)[:, :, KC * w:KC * w + KC],
                        scalar=hg[:, 0, 1, bass.ds(dt, 1), w:w + 1].rearrange("p a b -> p (a b)"), in1=xv,
                        op0=ALU.mult, op1=ALU.add)
                last.then_inc(x_ready[s], 1)

            blocks(dve, "glu", split_lo, glu)

        def s5_pool(pool):
            m = 0
            pool.wait_ge(hh_ready, pieces_before(2))
            pool.memset(Hs[:, :, :, :, 0:1].rearrange("p a b c d -> p (a b c) d"), 0.0).then_inc(H_zero, 1)
            for b in range(NB5):
                s = b % 2
                pool.wait_ge(g_ready, 2 * b + 2)
                if b >= 2:
                    pool.wait_ge(Y_ready, b - 1)
                ec, es = etS[:, s, 0, :, :], etS[:, s, 1, :, :]
                gre, gim = (gr[:, r, :].rearrange("p (g k) -> p g k", k=NK) for r in range(2))
                hre, him = Hs[:, s, 0, :, 1:NK + 1], Hs[:, s, 1, :, 1:NK + 1]
                for a, c, e, f, dst, op in ((gre, ec, gim, es, hre, ALU.subtract), (gre, es, gim, ec, him, ALU.add)):
                    pool.tensor_tensor(tc[:, :, :], a, c, ALU.mult).then_inc(q_step, 1)
                    pool.tensor_tensor(td[:, :, :], e, f, ALU.mult).then_inc(q_step, 1)
                    m += 2
                    pool.wait_ge(q_step, m)
                    pool.tensor_tensor(dst, tc[:, :, :], td[:, :, :], op).then_inc(q_step, 1)
                    m += 1
                    pool.wait_ge(q_step, m)
                pool.sem_inc(H_ready, 1)

        def s5_act(act):
            for b in range(NB5):
                act.wait_ge(Y_ready, b + 1)
                if b >= 2:
                    act.wait_ge(y_out, 16 * L * (b - 1))
                y = PS[:, 4 + 2 * (b % 2):6 + 2 * (b % 2), 0:GPB * NK].rearrange("p g (r k) -> p r g k", k=NK)
                act.activation(Yt[:, b % 2, :, :].rearrange("p (r g) k -> p r g k", g=2), y, ACT.Copy).then_inc(Yt_ready, 1)
            for k in range(KT):
                act.wait_ge(y_in, 16 * (k + 1))
                act.activation(hS[:, k, :, :], hS[:, k, :, :], ACT.Gelu_apprx_tanh).then_inc(gelu_ready, 1)
            for k in range(KT):
                act.wait_ge(gelu_ready, k + 1)
                act.activation(hh[:, k, :], hS[:, k, :, :].rearrange("p s c -> p (s c)"), ACT.Copy).then_inc(zh_ready, 1)

            def gate(i, s):
                act.wait_ge(blk_done[s], 1 + BASE["glu"] // 2 + i + 1)
                act.activation(sil[:, s, :], PS[:, 2 + s, :], ACT.Sigmoid, bias=glub[:, 1, bass.ds(2 * i + s, 1)]).then_inc(sig_ready[s], 1)

            blocks(act, "glu", split_hi, gate)

        def glu_pe(pe):
            pe.wait_ge(zl_ready, KT)
            with pe.Fori(0, KT // 2) as i:
                for s in range(2):
                    pe.wait_ge(wlo_ready[s], 1 + BASE["glu"] // 2 + i + 1)
                    pe.wait_ge(glu_ready[s], 1 + i)
                    for ab in range(2):
                        for k in range(KT):
                            last = mm3(pe, PS[:, 2 * ab + s, :], s, (2 * k + ab) * P, hh[:, k, :], hl[:, k, :], k == 0, k == KT - 1)
                    last.then_inc(blk_done[s], 1)
        gst = ExitStack()
        pk = sb("pk", [P, 2, CTX + 4], F32, gst)
        pv = sb("pv", [P, 2, CTX + 4], F32, gst)
        pq = sb("pq", [P, 1, LAT + 4], F32, gst)
        ck = sb("ck", [P, 2, CTX], F32, gst)
        cv = sb("cv", [P, 2, CTX], F32, gst)
        cq = sb("cq", [P, 1, LAT], F32, gst)
        sqk = sb("sqk", [P, T], F32, gst)
        sqq = sb("sqq", [P, LAT], F32, gst)
        kn = sb("kn", [P, NCH, CH], F32, gst)
        qn = sb("qn", [P, 2, CH], F32, gst)
        vt = sb("vt", [P, NCH, CH], F32, gst)
        kd = sb("kd", [P, 2, NCH, CH], F32, gst)
        zg = sb("zg", [P, LAT], F32, gst)
        DTm = sb("DTm", [P, 2, NCH, CH], F32, gst)
        DTs = sb("DTs", [P, 2, NCH, CH], F32, gst)
        DTi = sb("DTi", [P, 2, 2, CH], F32, gst)
        NT = sb("NT", [P, 2, NCH, CH], F32, gst)
        NN = sb("NN", [P, 2, NCH, CH], F32, gst)
        X = sb("X", [P, 2, NCH, CH], F32, gst)
        BT = sb("BT", [P, 2, NCH, CH], F32, gst)
        BB = sb("BB", [P, 2, NCH, CH], F32, gst)
        EE = sb("EE", [P, 2, 3, NCH, CH], F32, gst)
        at = sb("at", [P, 2, 2, CH], F32, gst)
        S = sb("S", [P, 2, CH], F32, gst)
        r2 = sb("r2", [P, 2, CH], F32, gst)
        vn = sb("vn", [P, 2, CH], F32, gst)
        o1 = sb("o1", [P, 2, CH], F32, gst)
        oo = sb("oo", [P, 2, 2, CH], F32, gst)
        on = sb("on", [P, 2, CH], F32, gst)
        yt = sb("yt", [P, LAT], F32, gst)
        vec = sb("vec", [P, 6, NCH, 2, H], F32, gst)
        hv = sb("hv", [P, 6, NCH, 2], F32, gst)
        gw = sb("gw", [P, 10, NCH, 2 * H], F32, gst)
        etv = sb("etv", [P, NCH, 2], F32, gst)
        oss = sb("oss", [P, 4], F32, gst)
        convw = sb("convw", [P, H, 3, 5], F32, gst)
        gpar = sb("gpar", [P, 2, 2 * H], F32, gst)
        gng = sb("gng", [P, 1], F32, gst)
        yh = sb("yh", [P, KT, LAT], F32R, gst)
        yl = sb("yl", [P, KT, LAT], F32R, gst)
        gst.close()
        BETA, NBETA, GG, GC, EG, EK = range(6)

        PER = {"hv": 1, "pc": 3, "zg": 1, "conv": 15, "silu": 3, "square": 2, "sumsq": 2, "root": 2, "recip": 2, "kn": 2,
               "kT": 1, "vT": 1, "vt": 1, "kd": 2, "gram": 1, "gcB": 2, "dmin": 2, "dexp": 2, "mask": 6, "nt": 2, "at": 2,
               "ntT": 2, "nn": 2, "b0": 4, "x0": 2, "ee": 2, "prod": 20, "eva": 12, "evd": 20, "RS": 6, "r2": 6, "TV": 8,
               "vn": 8, "KV": 8, "S": 6, "o1": 4, "oo": 4, "osum": 1, "oss": 2, "oroot": 1, "orec": 1, "on": 1, "oT": 1,
               "yt": 1, "yh": 1, "yl": 1}
        gs_ = {n: sem("g_" + n) for n in PER}
        gp_in = sem("gp_in")
        gstep = sem("gstep")
        gact = sem("gact")
        gate_mm = sem("gate_mm")
        gate_done = sem("gate_done")
        gba_ready = sem("gba_ready")

        def need(eng, name, h, n):
            eng.wait_ge(gs_[name], PER[name] * h + n + (name in ("yt", "yl")))

        def told(ins, name):
            ins.then_inc(gs_[name], 1)

        ORDER = [(0, 1, 2, 3), (1, 0, 3, 2)]
        ACT_ROUNDS = [0, 1, 2, 4, 6, 8]

        def gates_pe(pe):
            pe.wait_ge(norm_done, pieces_before(5, ("ffn", "gdn")))
            pe.wait_ge(gba_ready, 2)
            for c in range(NCH):
                dst = PS[:, 7, 32 * c:32 * c + 32]
                for k in range(KT):
                    th, tl = hh[:, k, c * CH:(c + 1) * CH], hl[:, k, c * CH:(c + 1) * CH]
                    pe.matmul(dst, th, gwah[:, k, :], start=k == 0, stop=False)
                    pe.matmul(dst, tl, gwah[:, k, :], start=False, stop=False)
                    last = pe.matmul(dst, th, gwal[:, k, :], start=False, stop=k == KT - 1)
            last.then_inc(gate_mm, 1)
            pe.wait_ge(gstep, GATE_G)
            for c in range(NCH):
                for d in range(2):
                    at_ = 128 + 16 * c + 8 * d
                    pe.matmul(PS[:, 7, at_:at_ + 8], const(f"tri{d}"), vec[:, GG, c, d, :], start=True, stop=True)
                last = pe.matmul(PS[:, 7, 192 + 16 * c:208 + 16 * c], const("one"), vec[:, GG, c, :, :].rearrange("p a b -> p (a b)"),
                                 start=True, stop=True)
            last.then_inc(gate_mm, 1)

        def gates_act(act):
            raw_ba = PS[:, 7, 0:128].rearrange("p (c j) -> p c j", j=32)
            act.wait_ge(gp_in, 16 * 4)
            act.activation(gwah[:, :, :], gwa[:, :, :], ACT.Copy).then_inc(gba_ready, 1)
            act.wait_ge(gate_mm, 1)
            act.activation(vec[:, BETA, :, :, :].rearrange("p c d h -> p c (d h)"), raw_ba[:, :, 0:16], ACT.Sigmoid).then_inc(gact, 1)
            act.activation(gpar[:, 0, :], gpar[:, 0, :], ACT.Exp).then_inc(gact, 1)
            act.wait_ge(gstep, 2)
            act.activation(gw[:, 2, :, :], gw[:, 1, :, :], ACT.Exp).then_inc(gact, 1)
            act.wait_ge(gstep, 3)
            act.activation(gw[:, 4, :, :], gw[:, 3, :, :], ACT.Ln).then_inc(gact, 1)
            act.wait_ge(gstep, GATE_G + 3)
            act.activation(vec[:, EG, :, :, :].rearrange("p c d h -> p c (d h)"),
                           vec[:, GC, :, :, :].rearrange("p c d h -> p c (d h)"), ACT.Exp).then_inc(gact, 1)
            act.activation(vec[:, EK, :, :, :].rearrange("p c d h -> p c (d h)"), gw[:, 8, :, :], ACT.Exp).then_inc(gact, 1)
            act.activation(gw[:, 9, :, :], gw[:, 7, :, :], ACT.Exp).then_inc(gact, 1)

        def gates_dve(dve):
            n = [0]

            def step(ins):
                n[0] += 1
                ins.then_inc(gstep, 1)
                dve.wait_ge(gstep, n[0])

            raw_ba = PS[:, 7, 0:128].rearrange("p (c j) -> p c j", j=32)
            dtb = gpar[:, 1, :].unsqueeze(1).to_broadcast([P, NCH, 2 * H])
            ea = gpar[:, 0, :].unsqueeze(1).to_broadcast([P, NCH, 2 * H])
            dve.wait_ge(gba_ready, 1)
            dve.tensor_tensor(gwal[:, :, :], gwa[:, :, :], gwah[:, :, :].bitcast(F32), ALU.subtract).then_inc(gba_ready, 1)
            dve.wait_ge(gact, 1)
            a, na, e, u, ln, q, w, tot, rest = (gw[:, i, :, :] for i in range(9))
            step(dve.tensor_tensor(a, raw_ba[:, :, 16:32], dtb, ALU.add))
            step(dve.scalar_tensor_tensor(out=na, in0=a, scalar=-1.0, in1=a, op0=ALU.mult, op1=ALU.min))
            dve.wait_ge(gact, 3)
            step(dve.tensor_scalar(u, e, 1.0, None, ALU.add))
            step(dve.tensor_scalar(q, u, -1.0, None, ALU.add))
            step(dve.tensor_tensor(q, e, q, ALU.subtract))
            step(dve.reciprocal(w, u))
            step(dve.tensor_tensor(q, q, w, ALU.mult))
            dve.wait_ge(gact, 4)
            step(dve.tensor_tensor(q, q, ln, ALU.add))
            step(dve.scalar_tensor_tensor(out=q, in0=a, scalar=0.0, in1=q, op0=ALU.max, op1=ALU.add))
            g = vec[:, GG, :, :, :].rearrange("p c d h -> p c (d h)")
            step(dve.scalar_tensor_tensor(out=g, in0=q, scalar=-1.0, in1=ea, op0=ALU.mult, op1=ALU.mult))
            assert n[0] == GATE_G
            dve.wait_ge(gate_mm, 2)
            gc = vec[:, GC, :, :, :].rearrange("p c d h -> p c (d h)")
            step(dve.tensor_copy(gc, PS[:, 7, 128:192].rearrange("p (c j) -> p c j", j=16)))
            step(dve.tensor_copy(tot, PS[:, 7, 192:256].rearrange("p (c j) -> p c j", j=16)))
            step(dve.tensor_tensor(rest, tot, gc, ALU.subtract))
            step(dve.tensor_scalar(vec[:, NBETA, :, :, :].rearrange("p c d h -> p c (d h)"),
                                   vec[:, BETA, :, :, :].rearrange("p c d h -> p c (d h)"), -1.0, None, ALU.mult))
            for t in (pk, pv, pq):
                dve.memset(t[:, :, 0:2], 0.0)
                step(dve.memset(t[:, :, CTX + 2:CTX + 4], 0.0))
            dve.wait_ge(gact, 7)
            dve.sem_inc(gate_done, 1)

        def gdn_pe(pe):
            gates_pe(pe)
            pe.wait_ge(gate_done, 1)
            with pe.Fori(0, H) as h:
                pe.wait_ge(gs_["yt"], 1 + h)
                for s, c0 in ((0, 0), (1, CTX)):
                    pe.wait_ge(wlo_ready[s], 1 + BASE["gdn"] // 2 + h + 1)
                    for ab in range(2):
                        for k in range(KT):
                            last = mm3(pe, PS[:, 2 * s + ab, 0:T - c0], s, (2 * k + ab) * P, hh[:, k, c0:T], hl[:, k, c0:T],
                                       k == 0, k == KT - 1)
                    last.then_inc(blk_done[s], 1)
                need(pe, "hv", h, 1)
                for d in range(2):
                    for c in range(NCH):
                        last = pe.matmul(PS[:, 6 + d, c * CH:(c + 1) * CH], hv[:, GG, c, d:d + 1].to_broadcast([P, CH]),
                                         const(f"tri{d}"), start=True, stop=True)
                    told(last, "gcB")
                need(pe, "square", h, 1)
                told(pe.matmul(PS[:, 4, :], const("one"), sqk[:, :], start=True, stop=True), "sumsq")
                need(pe, "square", h, 2)
                told(pe.matmul(PS[:, 5, 0:LAT], const("one"), sqq[:, :], start=True, stop=True), "sumsq")
                need(pe, "kn", h, 1)
                for c in range(NCH):
                    last = pe.transpose(PS[:, 4, c * CH:(c + 1) * CH], kn[:, c, :], const("eye"))
                told(last, "kT")
                need(pe, "kn", h, 2)
                need(pe, "silu", h, 2)
                vf = cv[:, :, :].rearrange("p a t -> p (a t)")
                for c in range(NCH):
                    last = pe.transpose(PS[:, 5, c * CH:(c + 1) * CH], vf[:, c * CH:(c + 1) * CH], const("eye"))
                told(last, "vT")
                for c in range(NCH):
                    pe.matmul(PS[:, 0, c * CH:(c + 1) * CH], kn[:, c, :], kn[:, c, :], start=True, stop=True)
                for c in range(2):
                    last = pe.matmul(PS[:, 2, c * CH:(c + 1) * CH], kn[:, 2 + c, :], qn[:, c, :], start=True, stop=True)
                told(last, "gram")
                for d in range(2):
                    need(pe, "nt", h, d + 1)
                    for c in range(NCH):
                        last = pe.transpose(PS[:, 6 + d, c * CH:(c + 1) * CH], NT[:, d, c, :], const("eye"))
                    told(last, "ntT")
                need(pe, "zg", h, 1)
                need(pe, "vt", h, 1)
                need(pe, "kd", h, 2)
                for rnd in range(10):
                    for d in range(2):
                        banks = ((1, 3, 6), (4, 5, 7))[d]
                        if rnd == 0:
                            need(pe, "b0", h, 2 * d + 2)
                            need(pe, "nn", h, d + 1)
                            need(pe, "x0", h, d + 1)
                        else:
                            need(pe, "evd", h, 2 * (rnd - 1) + d + 1)
                            if rnd - 1 in ACT_ROUNDS:
                                need(pe, "eva", h, 2 * ACT_ROUNDS.index(rnd - 1) + d + 1)
                            if rnd == 4:
                                need(pe, "ee", h, d + 1)
                        todo = [[(BB, BT), (BT, BB)], [(BB, X), (BB, BT), (BT, BB)], [(BB, X), (BT, BB)], [(BB, X)]]
                        if rnd < 4:
                            for (lt, rt), bank in zip(todo[rnd], banks):
                                for c in range(NCH):
                                    last = pe.matmul(PS[:, bank, c * CH:(c + 1) * CH], lt[:, d, c, :], rt[:, d, c, :], start=True, stop=True)
                        elif rnd % 2 == 0:
                            for c in range(NCH):
                                pe.transpose(PS[:, banks[0], c * CH:(c + 1) * CH], X[:, d, c, :], const("eye"))
                            for c in range(NCH):
                                last = pe.matmul(PS[:, banks[1], c * CH:(c + 1) * CH], EE[:, d, (rnd - 4) // 2, c, :], X[:, d, c, :],
                                                 start=True, stop=True)
                        else:
                            for c in range(NCH):
                                last = pe.matmul(PS[:, banks[2], c * CH:(c + 1) * CH], BT[:, d, c, :], BB[:, d, c, :], start=True, stop=True)
                        told(last, "prod")
                for j in range(NCH):
                    for d in range(2):
                        c = ORDER[d][j]
                        if j:
                            need(pe, "S", h, 2 * (j - 1) + d + 1)
                            last = pe.matmul(PS[:, (1, 4)[d], 0:CH], kn[:, c, :], S[:, d, :], start=True, stop=True)
                            if c >= 2:
                                if j == 3:
                                    need(pe, "o1", h, d + 1)
                                last = pe.matmul(PS[:, 6 + d, 0:CH], qn[:, c - 2, :], S[:, d, :], start=True, stop=True)
                            told(last, "RS")
                    for d in range(2):
                        c = ORDER[d][j]
                        if j:
                            need(pe, "r2", h, 2 * (j - 1) + d + 1)
                            rhs = r2[:, d, :]
                        else:
                            need(pe, "evd", h, 19 + d)
                            rhs = vt[:, c, :]
                        told(pe.matmul(PS[:, (3, 5)[d], 0:CH], X[:, d, c, :], rhs, start=True, stop=True), "TV")
                    for d in range(2):
                        c = ORDER[d][j]
                        need(pe, "vn", h, 2 * j + d + 1)
                        if c >= 2:
                            last = pe.matmul(PS[:, (0, 2)[d], CH:2 * CH], at[:, d, c - 2, :], vn[:, d, :], start=True, stop=True)
                        if j < NCH - 1:
                            last = pe.matmul(PS[:, (0, 2)[d], 0:CH], kd[:, d, c, :], vn[:, d, :], start=True, stop=True)
                        told(last, "KV")
                need(pe, "on", h, 1)
                for c in range(2):
                    last = pe.transpose(PS[:, 6, c * CH:(c + 1) * CH], on[:, c, :], const("eye"))
                told(last, "oT")
            pe.wait_ge(gs_["yl"], 1 + H)
            with pe.Fori(0, COUNT["wo"] // 2) as i:
                for s in range(2):
                    pe.wait_ge(wlo_ready[s], 1 + BASE["wo"] // 2 + i + 1)
                    for ab in range(2):
                        pe.wait_ge(x_ready[ab], 1 + KT // 2 * 4 + 2 * i + s - 1)
                        for k in range(KT):
                            last = mm3(pe, PS[:, 2 * ab + s, 0:LAT], s, (2 * k + ab) * P, yh[:, k, :], yl[:, k, :], k == 0, k == KT - 1)
                    last.then_inc(blk_done[s], 1)

        def gdn_act(act):
            gates_act(act)
            u0 = BASE["gdn"] // 2
            with act.Fori(0, H) as h:
                split_hi(act, 1, u0 + h)
                act.wait_ge(blk_done[0], 1 + u0 + h + 1)
                for bank, t in ((0, pk), (1, pv)):
                    told(act.activation(t[:, :, 2:CTX + 2], PS[:, bank, :].rearrange("p (a t) -> p a t", a=2), ACT.Copy), "pc")
                split_hi(act, 0, u0 + h + 1)
                act.wait_ge(blk_done[1], 1 + u0 + h + 1)
                told(act.activation(pq[:, :, 2:LAT + 2], PS[:, 2:3, 0:LAT], ACT.Copy), "pc")
                told(act.activation(zg[:, :], PS[:, 3, 0:LAT], ACT.Silu), "zg")
                for j, t in enumerate((ck, cv, cq)):
                    need(act, "conv", h, 5 * j + 5)
                    told(act.activation(t[:, :, :], t[:, :, :], ACT.Silu), "silu")
                need(act, "silu", h, 1)
                told(act.activation(sqk[:, :], ck[:, :, :].rearrange("p a t -> p (a t)"), ACT.Square), "square")
                need(act, "silu", h, 3)
                told(act.activation(sqq[:, :], cq[:, 0, :], ACT.Square), "square")
                need(act, "sumsq", h, 1)
                told(act.activation(sqk[:, :], PS[:, 4, :], ACT.Sqrt, bias=epst[:, 0:1]), "root")
                need(act, "sumsq", h, 2)
                told(act.activation(sqq[:, :], PS[:, 5, 0:LAT], ACT.Sqrt, bias=epst[:, 0:1]), "root")
                for d in range(2):
                    need(act, "dmin", h, d + 1)
                    told(act.activation(DTm[:, d, :, :], DTm[:, d, :, :], ACT.Exp), "dexp")
                need(act, "vT", h, 1)
                told(act.activation(vt[:, :, :].rearrange("p c t -> p (c t)"), PS[:, 5, :], ACT.Copy), "vt")
                for d in range(2):
                    need(act, "ntT", h, d + 1)
                    told(act.activation(NN[:, d, :, :].rearrange("p c t -> p (c t)"), PS[:, 6 + d, :], ACT.Copy), "nn")
                for n, rnd in enumerate(ACT_ROUNDS):
                    for d in range(2):
                        banks = ((1, 3, 6), (4, 5, 7))[d]
                        need(act, "prod", h, 2 * rnd + d + 1)
                        copies = {0: [(BT, 0)], 1: [(BT, 1), (BB, 2)], 2: [(BB, 1)]}.get(rnd, [(BT, 0)])
                        for t, b in copies:
                            last = act.activation(t[:, d, :, :].rearrange("p c t -> p (c t)"), PS[:, banks[b], :], ACT.Copy)
                        told(last, "eva")
                for j in range(2, NCH):
                    for d in range(2):
                        c = ORDER[d][j]
                        need(act, "RS", h, 2 * (j - 1) + d + 1)
                        if j == 3:
                            need(act, "oo", h, d + 1)
                        told(act.activation(o1[:, d, :], PS[:, 6 + d, 0:CH], ACT.Copy, scale=hv[:, EG, c, d:d + 1]), "o1")
                need(act, "osum", h, 1)
                for c in range(2):
                    told(act.activation(on[:, c, :], oo[:, 0, c, :], ACT.Square, accum_out=oss[:, c:c + 1]), "oss")
                need(act, "oss", h, 2)
                told(act.activation(oss[:, 2:4], oss[:, 0:2], ACT.Sqrt, scale=1.0 / CH, bias=epst[:, 0:1]), "oroot")
            blocks(act, "wo", split_hi, lambda i, s: None)

        def gdn_dve(dve):
            gates_dve(dve)
            u0 = BASE["gdn"] // 2
            with dve.Fori(0, H) as h:
                dve.tensor_copy(hv[:, :, :, :].rearrange("p a c d -> p (a c d)").unsqueeze(2),
                                vec[:, :, :, :, bass.ds(h, 1)].rearrange("p a c d h -> p (a c d) h"))
                told(dve.tensor_copy(etv[:, :, :].rearrange("p c d -> p (c d)").unsqueeze(2),
                                     gw[:, 9, :, :].rearrange("p c (d h) -> p (c d) h", h=H)[:, :, bass.ds(h, 1)]), "hv")
                need(dve, "hv", h, 1)
                split_lo(dve, 1, u0 + h)
                for d in range(2):
                    need(dve, "gcB", h, d + 1)
                    for c in range(NCH):
                        last = dve.tensor_scalar(DTm[:, d, c, :], PS[:, 6 + d, c * CH:(c + 1) * CH], hv[:, GC, c, d:d + 1], 0.0,
                                                 ALU.subtract, ALU.min)
                    told(last, "dmin")

                def conv(src, dst, which, n):
                    need(dve, "pc", h, n + 1)
                    for tap in range(5):
                        w = convw[:, bass.ds(h, 1), which, tap:tap + 1].rearrange("p a b -> p (a b)")
                        win = src[:, :, tap:tap + CTX]
                        if tap == 0:
                            told(dve.tensor_scalar(dst[:, :, :], win, w, None, ALU.mult), "conv")
                        else:
                            need(dve, "conv", h, 5 * n + tap)
                            told(dve.scalar_tensor_tensor(out=dst[:, :, :], in0=win, scalar=w, in1=dst[:, :, :], op0=ALU.mult, op1=ALU.add),
                                 "conv")

                conv(pk, ck, 1, 0)
                conv(pv, cv, 2, 1)
                split_lo(dve, 0, u0 + h + 1)
                conv(pq, cq, 0, 2)
                need(dve, "root", h, 1)
                told(dve.reciprocal(sqk[:, :], sqk[:, :]), "recip")
                need(dve, "recip", h, 1)
                told(dve.tensor_tensor(kn[:, :, :].rearrange("p c t -> p (c t)"), ck[:, :, :].rearrange("p a t -> p (a t)"), sqk[:, :], ALU.mult),
                     "kn")
                need(dve, "root", h, 2)
                told(dve.reciprocal(sqq[:, :], sqq[:, :]), "recip")
                need(dve, "recip", h, 2)
                told(dve.scalar_tensor_tensor(out=qn[:, :, :].rearrange("p c t -> p (c t)"), in0=cq[:, 0, :], scalar=float(CH) ** -0.5,
                                              in1=sqq[:, :], op0=ALU.mult, op1=ALU.mult), "kn")
                need(dve, "kT", h, 1)
                for d in range(2):
                    told(dve.tensor_tensor(kd[:, d, :, :], PS[:, 4, :].rearrange("p (c t) -> p c t", c=NCH),
                                           hv[:, EK, :, d:d + 1].to_broadcast([P, NCH, CH]), ALU.mult), "kd")
                need(dve, "gram", h, 1)
                for d in range(2):
                    need(dve, "mask", h, 3 * d + 3)
                    told(dve.tensor_tensor(NT[:, d, :, :], PS[:, 0, :].rearrange("p (c t) -> p c t", c=NCH), DTs[:, d, :, :], ALU.mult), "nt")
                for d in range(2):
                    need(dve, "nt", h, d + 1)
                    told(dve.tensor_tensor(BT[:, d, :, :], NT[:, d, :, :], const("bd16").unsqueeze(1).to_broadcast([P, NCH, CH]), ALU.mult), "b0")
                    need(dve, "nn", h, d + 1)
                    told(dve.tensor_tensor(BB[:, d, :, :], NN[:, d, :, :], const("bd16").unsqueeze(1).to_broadcast([P, NCH, CH]), ALU.mult), "b0")
                for d in range(2):
                    told(dve.tensor_tensor(at[:, d, :, :], PS[:, 2, 0:2 * CH].rearrange("p (c t) -> p c t", c=2), DTi[:, d, :, :], ALU.mult), "at")
                for rnd in range(10):
                    for d in range(2):
                        banks = ((1, 3, 6), (4, 5, 7))[d]
                        need(dve, "prod", h, 2 * rnd + d + 1)
                        xd = X[:, d, :, :].rearrange("p c t -> p (c t)")
                        bd = BB[:, d, :, :].rearrange("p c t -> p (c t)")
                        if rnd == 0 or (rnd >= 4 and rnd % 2 == 0):
                            last = dve.tensor_copy(bd, PS[:, banks[1], :])
                        else:
                            bank = banks[0] if rnd < 4 else banks[2]
                            last = dve.tensor_tensor(xd, xd, PS[:, bank, :], ALU.add)
                        told(last, "evd")
                for j in range(NCH):
                    for d in range(2):
                        c = ORDER[d][j]
                        if j:
                            need(dve, "RS", h, 2 * (j - 1) + d + 1)
                            dve.scalar_tensor_tensor(out=r2[:, d, :], in0=PS[:, (1, 4)[d], 0:CH], scalar=hv[:, EG, c, d:d + 1],
                                                     in1=vt[:, c, :], op0=ALU.mult, op1=ALU.subtract).then_inc(gs_["r2"], 1)
                    for d in range(2):
                        c = ORDER[d][j]
                        need(dve, "TV", h, 2 * j + d + 1)
                        beta = hv[:, NBETA if j else BETA, c, d:d + 1]
                        told(dve.tensor_scalar(vn[:, d, :], PS[:, (3, 5)[d], 0:CH], beta, None, ALU.mult), "vn")
                    for d in range(2):
                        c = ORDER[d][j]
                        need(dve, "KV", h, 2 * j + d + 1)
                        if j == 0:
                            told(dve.tensor_copy(S[:, d, :], PS[:, (0, 2)[d], 0:CH]), "S")
                        elif j < NCH - 1:
                            told(dve.scalar_tensor_tensor(out=S[:, d, :], in0=S[:, d, :], scalar=etv[:, c, d:d + 1],
                                                          in1=PS[:, (0, 2)[d], 0:CH], op0=ALU.mult, op1=ALU.add), "S")
                        if c >= 2:
                            need(dve, "o1", h, 2 * (j - 2) + d + 1)
                            told(dve.tensor_tensor(oo[:, d, c - 2, :], o1[:, d, :], PS[:, (0, 2)[d], CH:2 * CH], ALU.add), "oo")
                need(dve, "oo", h, 4)
                told(dve.tensor_tensor(oo[:, 0, :, :], oo[:, 0, :, :], oo[:, 1, :, :], ALU.add), "osum")
                need(dve, "oroot", h, 1)
                told(dve.reciprocal(oss[:, 0:2], oss[:, 2:4]), "orec")
                need(dve, "orec", h, 1)
                for c in range(2):
                    last = dve.tensor_scalar(on[:, c, :], oo[:, 0, c, :], oss[:, c:c + 1], None, ALU.mult)
                told(last, "on")
                need(dve, "oT", h, 1)
                dve.wait_ge(gs_["yl"], 1 + h)
                told(dve.scalar_tensor_tensor(out=yt[:, :], in0=PS[:, 6, 0:LAT], scalar=gng[:, 0:1], in1=zg[:, :],
                                              op0=ALU.mult, op1=ALU.mult), "yt")

            def update(i, s):
                for ab in range(2):
                    dve.wait_ge(blk_done[s], 1 + BASE["wo"] // 2 + i + 1)
                    add_to_x(dve, 1, 1, 2 * (2 * i + s) + ab, CTX, 2 * ab + s, "turned").then_inc(x_ready[ab], 1)

            blocks(dve, "wo", split_lo, update)

        def gdn_pool(pool):
            pool.wait_ge(gate_done, 1)
            with pool.Fori(0, H) as h:
                for d in range(2):
                    need(pool, "dexp", h, d + 1)
                    tri = const(f"tri{d}").unsqueeze(1).to_broadcast([P, 2, CH])
                    strict = const(f"strict{d}").unsqueeze(1).to_broadcast([P, NCH, CH])
                    told(pool.tensor_tensor(DTi[:, d, :, :], DTm[:, d, 2:4, :], tri, ALU.mult), "mask")
                    told(pool.tensor_tensor(DTs[:, d, :, :], DTm[:, d, :, :], strict, ALU.mult), "mask")
                    need(pool, "mask", h, 3 * d + 2)
                    told(pool.tensor_tensor(DTs[:, d, :, :], DTs[:, d, :, :], hv[:, NBETA, :, d:d + 1].to_broadcast([P, NCH, CH]), ALU.mult),
                         "mask")
                for d in range(2):
                    need(pool, "b0", h, 2 * d + 1)
                    told(pool.tensor_tensor(X[:, d, :, :], BT[:, d, :, :], const("eye").unsqueeze(1).to_broadcast([P, NCH, CH]), ALU.add), "x0")
                for d in range(2):
                    need(pool, "nn", h, d + 1)
                    for n, name in enumerate(("e32", "e64", "e128")):
                        last = pool.tensor_tensor(EE[:, d, n, :, :], NN[:, d, :, :], const(name).unsqueeze(1).to_broadcast([P, NCH, CH]), ALU.mult)
                    told(last, "ee")
                need(pool, "yt", h, 1)
                told(pool.tensor_copy(yh[:, bass.ds(h, 1), :], yt[:, :].unsqueeze(1)), "yh")
                need(pool, "yh", h, 1)
                told(pool.tensor_tensor(yl[:, bass.ds(h, 1), :], yt[:, :].unsqueeze(1), yh[:, bass.ds(h, 1), :].bitcast(F32), ALU.subtract), "yl")


        block = ctx.enter_context(nc.Block())

        def prime(eng, *sems):
            for group in sems:
                for one in group:
                    eng.sem_inc(one, 1)

        @block.sync
        def _(sp):
            for dst, src in ((x[:, :, :], A["x"]), (consts[:, :, :], A["consts"]), (cvec[:, :, :], A["cvec"]),
                             (ng[:, :, :, :], A["norm_g"]), (fg[:, :], A["final_g"]), (modb[:, :, :], A["mod_b"])):
                sp.dma_start(dst, src).then_inc(par_in, 16)
            if "s5" in STAGES:
                for dst, src in ((s5p[:, :, :], A["s5_a"]), (sB[:, :, :, :], A["s5_b"]), (sC[:, :, :, :], A["s5_c"]), (sd[:, :], A["s5_d"])):
                    sp.dma_start(dst, src).then_inc(s5_par, 16)
                sp.dma_start(glub[:, :, :], A["glu_b"]).then_inc(s5_par, 16)
                prep_sp(sp)
                for s_, n in ((et_out, 1), (cx_out, NB5), (vw_out, NB5), (z_out, NB5)):
                    sp.wait_ge(s_, 16 * n)
            for layer in range(2):
                with sp.Fori(0, MB // MS) as i:
                    for s in range(MS):
                        sp.wait_ge(mod_used[s], 1 + MB // MS * layer + i)
                        sp.dma_start(modw[:, s, :, :], A["mod_w"][layer, bass.ds(MS * i + s, 1)].rearrange("a p k n -> (a p) k n"))\
                            .then_inc(mod_in[s], 16)
            for name, _, _ in PHASES:
                if name == "glu":
                    load_blocks(sp, name, 0, 1)
                    s5_sp(sp)
                    load_blocks(sp, name, 1)
                elif name == "gdn":
                    load_blocks(sp, name, 0, 1)
                    for s in range(2):
                        sp.wait_ge(x_ready[s], 1 + KT // 2 * 4)
                    for dst, src in ((gwa[:, :, :], A["g_w"]), (convw[:, :, :, :], A["g_conv"]), (gpar[:, :, :], A["g_par"]), (gng[:, :], A["g_ng"])):
                        sp.dma_start(dst, src).then_inc(gp_in, 16)
                    load_blocks(sp, name, 1)
                else:
                    load_blocks(sp, name)
            if "final" in STAGES:
                sp.wait_ge(fin_ready, KT)
                sp.dma_start(out, tmp[:, :, CTX:T]).then_inc(out_done, 16)
            else:
                for q in range(2):
                    sp.wait_ge(x_ready[q], 1 + KT // 2 * len(NORMS))
                sp.dma_start(out, x[:, :, :]).then_inc(out_done, 16)
            sp.wait_ge(out_done, 16)

        @block.scalar
        def _(act):
            act.wait_ge(par_in, 16 * NPAR)
            act.activation(cvec[:, :, :], cvec[:, :, :], ACT.Silu).then_inc(silu_c, 1)
            if "s5" in STAGES:
                prep_act(act)
            split_hi(act, 0, 0)
            norm_act(act, 0)
            ffn_act(act, 0)
            if "s5" in STAGES:
                norm_act(act, 1)
                s5_act(act)
                norm_act(act, 2)
                ffn_act(act, 1)
            if "gdn" in STAGES:
                norm_act(act, 3)
                ffn_act(act, 2)
                norm_act(act, 4)
                gdn_act(act)
                norm_act(act, 5)
                ffn_act(act, 3)
            if "final" in STAGES:
                norm_act(act, 6)

        @block.tensor
        def _(pe):
            prime(pe, blk_done, mod_used)
            if "s5" in STAGES:
                prep_pe(pe)
            mods_pe(pe)
            norm_pe(pe, 0)
            ffn_pe(pe, 0)
            if "s5" in STAGES:
                norm_pe(pe, 1)
                s5_pe(pe)
                glu_pe(pe)
                norm_pe(pe, 2)
                ffn_pe(pe, 1)
            if "gdn" in STAGES:
                norm_pe(pe, 3)
                ffn_pe(pe, 2)
                norm_pe(pe, 4)
                gdn_pe(pe)
                norm_pe(pe, 5)
                ffn_pe(pe, 3)
            if "final" in STAGES:
                norm_pe(pe, 6)

        @block.vector
        def _(dve):
            prime(dve, wlo_ready, gt_ready, x_ready, glu_ready, [gs_["yt"]])
            if "s5" in STAGES:
                prep_dve(dve)
            mods_dve(dve)
            split_lo(dve, 0, 0)
            norm_dve(dve, 0)
            ffn_dve(dve, 0)
            if "s5" in STAGES:
                norm_dve(dve, 1)
                s5_dve(dve)
                norm_dve(dve, 2)
                ffn_dve(dve, 1)
            if "gdn" in STAGES:
                norm_dve(dve, 3)
                ffn_dve(dve, 2)
                norm_dve(dve, 4)
                gdn_dve(dve)
                norm_dve(dve, 5)
                ffn_dve(dve, 3)
            if "final" in STAGES:
                final_dve(dve)

        @block.gpsimd
        def _(pool):
            prime(pool, hid_ready, [gs_["yl"]])
            ffn_pool(pool, 0)
            if "s5" in STAGES:
                s5_pool(pool)
                ffn_pool(pool, 1)
            if "gdn" in STAGES:
                ffn_pool(pool, 2)
                gdn_pool(pool)
                ffn_pool(pool, 3)


def constants():
    r, c = np.arange(P)[:, None], np.arange(P)[None, :]
    same = {b: r // b == c // b for b in (16, 32, 64, 128)}
    made = {"mean": np.full((P, P), 1.0 / D), "one": np.ones((P, P)), "eye": r == c,
            "tri0": r <= c, "tri1": r >= c, "strict0": r < c, "strict1": r > c, "bd16": same[16],
            "m16": r % C16 == c, "e32": same[32] & ~same[16], "e64": same[64] & ~same[32], "e128": same[128] & ~same[64]}
    return np.stack([np.asarray(made[n], np.float32) for n in CONSTS], axis=1)


def tiles(v):
    v = np.asarray(v)
    return np.moveaxis(v.reshape(*v.shape[:-1], KT, P), -1, 0)


def weight_blocks(w, cut):
    k, n = w.shape[0] // P, w.shape[1]
    t = w.reshape(k, P, n // P, P)
    return np.stack([t[:, :, c, :].transpose(1, 0, 2, 3).reshape(P, -1) for c in cut])


def layout_s5(I):
    def states(a):
        n = a.ndim
        a = a.reshape(2, PR, 2, 64, *a.shape[3:])
        return a.transpose(2, 3, 1, 0, *range(4, n + 1)).reshape(P, 64, *a.shape[4:])

    dt = np.broadcast_to(I["s5_log_dt"][0][:, :, None], (2, G, 64))
    b = np.stack([I["s5_b_re"][0], I["s5_b_im"][0]], axis=3)
    c = np.stack([I["s5_c_re"][0], I["s5_c_im"][0]], axis=3).transpose(0, 1, 4, 3, 2)
    return {"s5_a": np.stack([states(I["s5_a_re"][0]), states(I["s5_a_im"][0]), states(dt)], axis=1),
            "s5_b": states(b), "s5_c": states(c), "s5_d": tiles(I["s5_d"][0]),
            "glu_b": tiles(I["s5_glu_b"][0].reshape(2, D)),
            "w_glu": weight_blocks(I["s5_glu_w"][0], [[j, KT + j] for j in range(KT)])}


def layout_gdn(I):
    w = I["gdn_w_in"][0]
    conv = I["gdn_conv_w"][0].reshape(5, 3, H, P).transpose(3, 2, 1, 0)
    par = np.stack([I["gdn_a_log"][0].reshape(2 * H), I["gdn_dt_bias"][0].reshape(2 * H)])
    return {"w_gdn": weight_blocks(w[:, :4 * D], [c for h in range(H) for c in ([H + h, 2 * H + h], [h, 3 * H + h])]),
            "w_wo": weight_blocks(I["gdn_w_out"][0], [[2 * j, 2 * j + 1] for j in range(KT // 2)]),
            "g_w": w[:, 4 * D:].reshape(KT, P, 4 * H).transpose(1, 0, 2), "g_conv": conv,
            "g_par": np.broadcast_to(par, (P, 2, 2 * H)), "g_ng": I["gdn_norm_g"][0].reshape(P, 1)}


def layout(inputs):
    I = {n: np.asarray(v) for n, v in inputs.items()}
    a = {"x": np.ascontiguousarray(tiles(np.concatenate([I["ctx"][0], I["x"][0]], axis=0)).transpose(0, 2, 1)),
         "consts": constants(),
         "cvec": np.stack([tiles(I["c_ctx"]), tiles(I["c"][0])], axis=-1),
         "norm_g": tiles(I["norm_g"]), "final_g": tiles(I["final_g"]),
         "mod_b": I["mod_b"].reshape(2, NMOD * KT, P).transpose(2, 0, 1),
         "mod_w": I["mod_w"].reshape(2, KT, P, MB, 256).transpose(0, 3, 2, 1, 4)}
    for f in range(4):
        w13, w2 = I["ffn_w13"][f // 2, f % 2], I["ffn_w2"][f // 2, f % 2]
        if f"f{f}a" not in COUNT:
            continue
        a[f"w_f{f}a"] = weight_blocks(w13, [[j, FT + j] for j in range(FT)])
        t = w2.reshape(2, FH, P, KT, P)
        a[f"w_f{f}b"] = t.transpose(3, 0, 2, 1, 4).reshape(2 * KT, P, FH * P)
    if "s5" in STAGES:
        a.update(layout_s5(I))
    if "gdn" in STAGES:
        a.update(layout_gdn(I))
    return {n: np.ascontiguousarray(v) for n, v in a.items()}


STAGES = ("s5", "gdn", "final")


def kernel(**inputs):
    from concourse import bacc
    from concourse.bass_utils import run_bass_kernel_spmd

    nc = bacc.Bacc("TRN2", target_bir_lowering=False, num_devices=1)
    arrays = layout(inputs)
    aps = {n: nc.dram_tensor("in_" + n, v.shape, F32, kind="ExternalInput").ap() for n, v in arrays.items()}
    out = nc.dram_tensor("out_0", (P, KT, LAT), F32, kind="ExternalOutput").ap()
    program(nc, aps, out)
    r = run_bass_kernel_spmd(nc, [{"in_" + n: v for n, v in arrays.items()}], core_ids=[0])
    y = r.results[0]["out_0"]
    return np.ascontiguousarray(y.transpose(2, 1, 0).reshape(1, LAT, D))
```

```python
from contextlib import ExitStack

import numpy as np

import concourse.bass as bass
from concourse import mybir

F32 = mybir.dt.float32
F32R = mybir.dt.float32r
ACT = mybir.ActivationFunctionType
ALU = mybir.AluOpType

P = 128
D = 1024
KT = D // P
CTX = 256
LAT = 256
T = CTX + LAT
FF = 2816
FT = FF // P
FH = FT // 2
NMOD = 9
EPS = 1e-6
GRID_W = 64
ROWS = LAT // GRID_W
BLK = 2048

G = 64
PR = G // 2
C16 = 16
L = 8
NK = T // L
KC = CTX // L
GPB = 4
NB5 = PR // GPB
S5_PARTS = [(0, 2), (2, KT)]
ZW = 2 * L - 1

H = 8
CH = 128
NCH = T // CH

PHASES = [("f0a", FT, BLK), ("f0b", 2 * KT, FH * P), ("glu", KT, BLK), ("f1a", FT, BLK), ("f1b", 2 * KT, FH * P),
          ("f2a", FT, BLK), ("f2b", 2 * KT, FH * P), ("gdn", 2 * H, BLK), ("wo", KT // 2, BLK),
          ("f3a", FT, BLK), ("f3b", 2 * KT, FH * P)]
BASE = {}
_at = 0
for _n, _b, _c in PHASES:
    BASE[_n] = _at
    _at += _b
BLOCKS = _at
COUNT = {n: b for n, b, _ in PHASES}
COLS = {n: c for n, _, c in PHASES}

MS = 3
MB = NMOD * KT
MU = 2 * MS
MHEAD = MB // MU - 7

CONSTS = ["mean", "one", "eye", "tri0", "tri1", "strict0", "strict1", "bd16", "e32", "e64", "e128", "m16"]

NORMS = [(0, 0, 0, "ffn"), (0, 1, 0, "s5"), (0, 2, 0, "ffn"), (1, 0, 0, "ffn"), (1, 1, 0, "gdn"), (1, 2, CTX, "ffn")]
NORM_OF_FFN = [0, 2, 3, 5]
X_STAGE_OF_FFN = [0, 2, 3, 5]
SUM_STEPS = 1 + 2 * (KT - 2)
PIECES = [(2 if c0 == 0 else 1) * KT for _, _, c0, _ in NORMS]


def pieces_before(m, of=("ffn", "s5", "gdn")):
    return sum(p for p, (_, _, _, k) in zip(PIECES[:m], NORMS[:m]) if k in of)

TWO_PI = [6.28125, 0.0019350051879882812, 3.01991598196e-07]
PREP_ANGLE = 8
GATE_G = 10


def program(nc, A, out):
    ctx = ExitStack()
    with ctx:
        def sem(name):
            return ctx.enter_context(nc.semaphore(name))

        def pair(name):
            return [sem(f"{name}{i}") for i in range(2)]

        def sb(name, shape, dt=F32, stack=None):
            return (stack or ctx).enter_context(nc.sbuf_tensor(name, shape, dt))

        x = sb("x", [P, KT, T])
        raw = sb("raw", [P, 2, BLK])
        whi = sb("whi", [P, 2, BLK], F32R)
        wlo = sb("wlo", [P, 2, BLK], F32R)
        consts = sb("consts", [P, len(CONSTS), P])
        mods = sb("mods", [P, 2, NMOD * KT, 2])
        gs = sb("gs", [P, 2, 3, KT, 2])
        hg = sb("hg", [P, 2, 3, KT, 2])
        ng = sb("ng", [P, 2, 3, KT])
        fg = sb("fg", [P, KT])
        rstd = sb("rstd", [P, T])
        std = sb("std", [P, T])
        epst = sb("epst", [P, 1])
        glub = sb("glub", [P, 2, KT])
        modb = sb("modb", [P, 2, NMOD * KT])
        gwa = sb("gwa", [P, KT, 4 * H])
        gwah = sb("gwah", [P, KT, 4 * H], F32R)
        gwal = sb("gwal", [P, KT, 4 * H], F32R)
        cvec = sb("cvec", [P, KT, 2])
        PS = ctx.enter_context(nc.psum_tensor("PS", [P, 8, 512], F32))

        def const(name):
            return consts[:, CONSTS.index(name), :]

        ffn = ExitStack()
        hidh = sb("hidh", [P, FT, T], F32R, ffn)
        hidl = sb("hidl", [P, FT, T], F32R, ffn)
        sil = sb("sil", [P, 2, T], F32, ffn)
        gt = sb("gt", [P, 2, T], F32, ffn)
        hh = sb("hh", [P, KT, T], F32R, ffn)
        hl = sb("hl", [P, KT, T], F32R, ffn)
        ffn.close()
        nrm = ExitStack()
        tmp = sb("tmp", [P, KT, T], F32, nrm)
        nrm.close()

        par_in = sem("par_in")
        NPAR = 4
        c_in = sem("c_in")
        mod_in = [sem(f"mod_in{s}") for s in range(MS)]
        mod_used = [sem(f"mod_used{s}") for s in range(MS)]
        mod_rows = sem("mod_rows")
        mod_turned = sem("mod_turned")
        silu_c = sem("silu_c")
        mods_ready = sem("mods_ready")
        raw_in = pair("raw_in")
        whi_ready = pair("whi_ready")
        wlo_ready = pair("wlo_ready")
        blk_done = pair("blk_done")
        sum_step = sem("sum_step")
        sq_ready = sem("sq_ready")
        ss_ready = sem("ss_ready")
        std_ready = sem("std_ready")
        rstd_ready = sem("rstd_ready")
        nt_ready = sem("nt_ready")
        hh_ready = sem("hh_ready")
        norm_done = sem("norm_done")
        sil_ready = pair("sil_ready")
        gt_ready = pair("gt_ready")
        hidh_ready = pair("hidh_ready")
        hid_ready = pair("hid_ready")
        x_ready = pair("x_ready")
        out_done = sem("out_done")
        fin_ready = sem("fin_ready")

        def mm3(pe, dst, slot, c, xh, xl, first, last):
            w_h, w_l = whi[:, slot, c:c + P], wlo[:, slot, c:c + P]
            pe.matmul(dst, w_h, xh, start=first, stop=False)
            pe.matmul(dst, w_h, xl, start=False, stop=False)
            return pe.matmul(dst, w_l, xh, start=False, stop=last)

        def load_blocks(sp, name, first=0, end=None):
            with sp.Fori(first, COUNT[name] // 2 if end is None else end) as i:
                for s in range(2):
                    use = BASE[name] // 2 + i
                    sp.wait_ge(wlo_ready[s], 1 + use)
                    sp.dma_start(raw[:, s, 0:COLS[name]], A["w_" + name][bass.ds(2 * i + s, 1)].rearrange("a p n -> (a p) n"))\
                        .then_inc(raw_in[s], 16)

        def split_hi(act, s, use):
            act.wait_ge(raw_in[s], 16 * use + 16)
            act.wait_ge(blk_done[s], 1 + use)
            act.activation(whi[:, s, :], raw[:, s, :], ACT.Copy).then_inc(whi_ready[s], 1)

        def split_lo(dve, s, use):
            dve.wait_ge(whi_ready[s], use + 1)
            dve.tensor_tensor(wlo[:, s, :], raw[:, s, :], whi[:, s, :].bitcast(F32), ALU.subtract)\
                .then_inc(wlo_ready[s], 1)

        def blocks(eng, name, split, work, start=0):
            n, u0 = COUNT[name] // 2, BASE[name] // 2
            whole = n - (BASE[name] + COUNT[name] == BLOCKS)
            with eng.Fori(0, whole) as i:
                split(eng, 1, u0 + i)
                work(i, 0)
                split(eng, 0, u0 + i + 1)
                work(i, 1)
            if whole < n:
                split(eng, 1, u0 + n - 1)
                work(n - 1, 0)
                work(n - 1, 1)

        def halves(c0):
            return [w for w in range(2) if w * CTX >= c0]

        def cols(w):
            return slice(CTX * w, CTX * w + CTX)

        def part(t, k, w, turned):
            v = t[:, bass.ds(k, 1), cols(w)]
            if w and turned:
                return v.rearrange("p a (c r) -> p (a r) c", r=ROWS)
            return v.rearrange("p a (r c) -> p (a r) c", r=ROWS)

        def s5_part(k, w):
            return hS[:, bass.ds(k, 1), :, KC * w:KC * w + KC].rearrange("p a s k -> p (a s) k")

        def natural_sk(t, k, w):
            return t[:, bass.ds(k, 1), cols(w)].rearrange("p a (k s) -> p (a s) k", s=L)

        def norm_act(act, m):
            layer, n, c0, feeds = NORMS[m] if m < len(NORMS) else (0, 0, CTX, "out")
            if m:
                for q in range(2):
                    act.wait_ge(x_ready[q], 1 + KT // 2 * m)
            else:
                act.wait_ge(mods_ready, 3)
                for stored, many in ((et_out, 2), (cx_out, NB5), (vw_out, NB5), (z_out, NB5)):
                    act.wait_ge(stored, 16 * many)
            act.activation(tmp[:, KT - 1, c0:T], x[:, KT - 1, c0:T], ACT.Square).then_inc(sq_ready, 1)
            act.wait_ge(ss_ready, m + 1)
            act.activation(std[:, c0:T], PS[:, 6, c0:T], ACT.Sqrt, bias=epst[:, 0:1]).then_inc(std_ready, 1)
            if feeds == "out":
                return
            b = pieces_before(m)
            with act.Fori(0, KT) as k:
                for j, w in enumerate(halves(c0)):
                    act.wait_ge(nt_ready, b + len(halves(c0)) * k + j + 1)
                    shift = mods[:, layer, bass.ds(3 * n * KT + k, 1), w:w + 1].rearrange("p a b -> p (a b)")
                    if feeds == "s5":
                        act.activation(s5_part(k, w), natural_sk(tmp, k, w), ACT.Identity, bias=shift).then_inc(hh_ready, 1)
                    else:
                        act.activation(part(hh, k, w, feeds == "gdn"), part(tmp, k, w, False), ACT.Identity,
                                       bias=shift).then_inc(hh_ready, 1)

        def norm_pe(pe, m):
            c0 = NORMS[m][2] if m < len(NORMS) else CTX
            pe.wait_ge(sum_step, SUM_STEPS * (m + 1))
            if m == 0:
                pe.wait_ge(mods_ready, 2)
            pe.matmul(PS[:, 6, c0:T], const("mean"), std[:, c0:T], start=True, stop=False)
            pe.wait_ge(sq_ready, m + 1)
            pe.matmul(PS[:, 6, c0:T], const("mean"), tmp[:, KT - 1, c0:T], start=False, stop=True).then_inc(ss_ready, 1)

        def squares_pool(pool, m):
            c0 = NORMS[m][2] if m < len(NORMS) else CTX
            u0 = 1 + KT // 2 * (m - 1)

            def updated(q, n):
                if m:
                    pool.wait_ge(x_ready[q], u0 + n)

            def square(dst, dt):
                xv = x[:, bass.ds(dt, 1), c0:T].rearrange("p a t -> p (a t)")
                pool.tensor_tensor(dst[:, c0:T], xv, xv, ALU.mult).then_inc(sum_step, 1)

            if m == 0:
                pool.wait_ge(par_in, 16 * NPAR)
            updated(0, 1)
            square(std, 0)
            with pool.Fori(0, KT // 2 - 1) as i:
                for q in range(2):
                    updated(1 - q, i + 1 + q)
                    square(rstd, 2 * i + 1 + q)
                    pool.wait_ge(sum_step, SUM_STEPS * m + 4 * i + 2 * q + 2)
                    pool.tensor_tensor(std[:, c0:T], std[:, c0:T], rstd[:, c0:T], ALU.add).then_inc(sum_step, 1)
                    pool.wait_ge(sum_step, SUM_STEPS * m + 4 * i + 2 * q + 3)

        def norm_dve(dve, m):
            layer, n, c0, feeds = NORMS[m]
            hs = halves(c0)
            dve.wait_ge(std_ready, m + 1)
            dve.reciprocal(rstd[:, c0:T], std[:, c0:T]).then_inc(rstd_ready, 1)
            dve.wait_ge(rstd_ready, m + 1)
            if m == 0:
                dve.wait_ge(mods_ready, 3)
            b = pieces_before(m)

            def scale(k):
                for w in hs:
                    dve.scalar_tensor_tensor(
                        out=tmp[:, bass.ds(k, 1), cols(w)].rearrange("p a t -> p (a t)"),
                        in0=x[:, bass.ds(k, 1), cols(w)].rearrange("p a t -> p (a t)"),
                        scalar=gs[:, layer, n, bass.ds(k, 1), w:w + 1].rearrange("p a b -> p (a b)"),
                        in1=rstd[:, cols(w)], op0=ALU.mult, op1=ALU.mult).then_inc(nt_ready, 1)

            def low_part(k):
                for j, w in enumerate(hs):
                    dve.wait_ge(hh_ready, b + len(hs) * k + j + 1)
                    dve.wait_ge(nt_ready, b + len(hs) * k + j + 1)
                    turned = feeds == "gdn"
                    dve.scalar_tensor_tensor(
                        out=part(hl, k, w, turned), in0=part(tmp, k, w, False),
                        scalar=mods[:, layer, bass.ds(3 * n * KT + k, 1), w:w + 1].rearrange("p a b -> p (a b)"),
                        in1=part(hh, k, w, turned).bitcast(F32), op0=ALU.add, op1=ALU.subtract).then_inc(norm_done, 1)

            if feeds == "s5":
                with dve.Fori(0, KT) as k:
                    scale(k)
                return
            scale(0)
            with dve.Fori(0, KT - 1) as k:
                scale(k + 1)
                low_part(k)
            low_part(KT - 1)

        def final_dve(dve):
            m = len(NORMS)
            dve.wait_ge(std_ready, m + 1)
            dve.reciprocal(rstd[:, CTX:T], std[:, CTX:T]).then_inc(rstd_ready, 1)
            dve.wait_ge(rstd_ready, m + 1)
            with dve.Fori(0, KT) as k:
                dve.scalar_tensor_tensor(
                    out=tmp[:, bass.ds(k, 1), CTX:T].rearrange("p a t -> p (a t)"),
                    in0=x[:, bass.ds(k, 1), CTX:T].rearrange("p a t -> p (a t)"), scalar=fg[:, bass.ds(k, 1)],
                    in1=rstd[:, CTX:T], op0=ALU.mult, op1=ALU.mult).then_inc(fin_ready, 1)

        def ffn_pe(pe, f):
            a, b, c0 = f"f{f}a", f"f{f}b", NORMS[NORM_OF_FFN[f]][2]
            made = pieces_before(NORM_OF_FFN[f], ("ffn", "gdn"))
            with pe.Fori(0, FT // 2) as i:
                for s in range(2):
                    pe.wait_ge(wlo_ready[s], 1 + BASE[a] // 2 + i + 1)
                    pe.wait_ge(gt_ready[s], 1 + FT // 2 * f + i)
                    for ab in range(2):
                        for k in range(KT):
                            if s == 0 and ab == 0:
                                pe.wait_ge(norm_done, made + len(halves(c0)) * (k + 1))
                            last = mm3(pe, PS[:, 2 * ab + s, c0:T], s, (2 * k + ab) * P, hh[:, k, c0:T], hl[:, k, c0:T],
                                       k == 0, k == KT - 1)
                    last.then_inc(blk_done[s], 1)
            for s in range(2):
                pe.wait_ge(hid_ready[s], FT // 2 * (f + 1))
            with pe.Fori(0, KT // 2) as i:
                for q in range(2):
                    pe.wait_ge(x_ready[q], 1 + KT // 2 * X_STAGE_OF_FFN[f] + i)
                    for s in range(2):
                        pe.wait_ge(wlo_ready[s], 1 + BASE[b] // 2 + 2 * i + q + 1)
                        for k in range(FH):
                            if s == 1 and k >= FH - 2:
                                pe.wait_ge(hid_ready[k - FH + 2], 1 + FT // 2 * (f + 1))
                            last = mm3(pe, PS[:, 4 + q, c0:T], s, k * P, hidh[:, FH * s + k, c0:T], hidl[:, FH * s + k, c0:T],
                                       s == 0 and k == 0, s == 1 and k == FH - 1)
                        last.then_inc(blk_done[s], 1)

        def ffn_act(act, f):
            a, b, c0 = f"f{f}a", f"f{f}b", NORMS[NORM_OF_FFN[f]][2]

            def silu(i, s):
                act.wait_ge(blk_done[s], 1 + BASE[a] // 2 + i + 1)
                act.activation(sil[:, s, c0:T], PS[:, s, c0:T], ACT.Silu).then_inc(sil_ready[s], 1)

            blocks(act, a, split_hi, silu)
            blocks(act, b, split_hi, lambda i, s: None)

        def ffn_dve(dve, f):
            a, b, c0 = f"f{f}a", f"f{f}b", NORMS[NORM_OF_FFN[f]][2]
            layer, n = NORMS[NORM_OF_FFN[f]][0:2]

            def gate(i, s):
                dve.wait_ge(sil_ready[s], FT // 2 * f + i + 1)
                dve.wait_ge(hid_ready[s], 1 + FT // 2 * f + i)
                dve.tensor_tensor(gt[:, s, c0:T], sil[:, s, c0:T], PS[:, 2 + s, c0:T], ALU.mult).then_inc(gt_ready[s], 1)

            blocks(dve, a, split_lo, gate)
            u0 = BASE[b] // 2

            def update(i, last_block):
                for q in range(2):
                    split_lo(dve, 1, u0 + 2 * i + q)
                    if not (last_block and q == 1):
                        split_lo(dve, 0, u0 + 2 * i + q + 1)
                    dve.wait_ge(blk_done[1], 1 + u0 + 2 * i + q + 1)
                    add_to_x(dve, layer, n, 2 * i + q, c0, 4 + q, None).then_inc(x_ready[q], 1)

            ends = BASE[b] + COUNT[b] == BLOCKS
            with dve.Fori(0, KT // 2 - ends) as i:
                update(i, False)
            if ends:
                update(KT // 2 - 1, True)

        def add_to_x(dve, layer, n, dt, c0, bank, order):
            for w in halves(c0):
                xv, pv = x[:, bass.ds(dt, 1), cols(w)], PS[:, bank, cols(w)]
                if order == "sk":
                    xv = xv.rearrange("p a (k s) -> p (a s) k", s=L)
                    pv = None
                elif order == "turned":
                    xv = xv.rearrange("p a (r c) -> p (a r) c", r=ROWS)
                    pv = PS[:, bank, 0:LAT].rearrange("p (c r) -> p r c", r=ROWS)
                else:
                    xv = xv.rearrange("p a t -> p (a t)")
                last = dve.scalar_tensor_tensor(
                    out=xv, in0=pv, scalar=hg[:, layer, n, bass.ds(dt, 1), w:w + 1].rearrange("p a b -> p (a b)"),
                    in1=xv, op0=ALU.mult, op1=ALU.add)
            return last

        def ffn_pool(pool, f):
            c0 = NORMS[NORM_OF_FFN[f]][2]
            with pool.Fori(0, FT // 2) as i:
                for s in range(2):
                    pool.wait_ge(gt_ready[s], 1 + FT // 2 * f + i + 1)
                    pool.tensor_copy(hidh[:, bass.ds(2 * i + s, 1), c0:T], gt[:, s:s + 1, c0:T]).then_inc(hidh_ready[s], 1)
                    pool.wait_ge(hidh_ready[s], FT // 2 * f + i + 1)
                    pool.tensor_tensor(hidl[:, bass.ds(2 * i + s, 1), c0:T], gt[:, s:s + 1, c0:T],
                                       hidh[:, bass.ds(2 * i + s, 1), c0:T].bitcast(F32), ALU.subtract)\
                        .then_inc(hid_ready[s], 1)

        def mods_pe(pe, first, end):
            def turn(it, q):
                pe.wait_ge(mod_rows, MU * it + q + 1)
                for h in range(2):
                    last = pe.matmul(PS[:, 6, bass.ds(4 * (MU * it + q) + 2 * h, 2)], rows[0:2, q % 2, h * P:(h + 1) * P], const("eye")[0:2, 0:2],
                                     start=True, stop=True)
                last.then_inc(mod_turned, 1)

            pe.wait_ge(silu_c, 1)
            with pe.Fori(first, end) as it:
                for q in range(MU):
                    pe.wait_ge(mod_in[q % MS], 16 * (2 * it + q // MS) + 16)
                    for k in range(KT):
                        last = pe.matmul(PS[0:2, 4 + q % 2, 0:256], cvec[:, k, :], modw[:, q % MS, k, :], start=k == 0, stop=k == KT - 1)
                    last.then_inc(mod_used[q % MS], 1)
                    if q:
                        turn(it, q - 1)
                turn(it, MU - 1)

        def mods_act(act, first, end):
            with act.Fori(first, end) as it:
                for q in range(MU):
                    act.wait_ge(mod_used[q % MS], 1 + 2 * it + q // MS + 1)
                    act.wait_ge(mod_turned, MU * it + q + 1)
                    act.activation(rows[0:2, q % 2, :], PS[0:2, 4 + q % 2, 0:256], ACT.Copy).then_inc(mod_rows, 1)

        def mods_dve(dve):
            dve.memset(epst[:, :], EPS).then_inc(mods_ready, 1)
            dve.wait_ge(par_in, 16 * NPAR)
            dve.wait_ge(mod_turned, MB + 2)
            dve.tensor_tensor(mods[:, :, :, :], PS[:, 6, 0:4 * NMOD * KT].rearrange("p (l a w) -> p l a w", l=2, w=2),
                              modb[:, :, :].unsqueeze(3).to_broadcast([P, 2, NMOD * KT, 2]), ALU.add).then_inc(mods_ready, 1)
            dve.wait_ge(mods_ready, 2)
            for layer in range(2):
                for n in range(3):
                    scale = mods[:, layer, (3 * n + 1) * KT:(3 * n + 2) * KT, :]
                    gate = mods[:, layer, (3 * n + 2) * KT:(3 * n + 3) * KT, :]
                    dve.scalar_tensor_tensor(out=gs[:, layer, n, :, :], in0=scale, scalar=1.0,
                                             in1=ng[:, layer, n, :].unsqueeze(2).to_broadcast([P, KT, 2]),
                                             op0=ALU.add, op1=ALU.mult)
                    last = dve.tensor_scalar(hg[:, layer, n, :, :], gate, 1.0 if n == 1 else 0.5, None, ALU.mult)
            last.then_inc(mods_ready, 1)
        prs = ExitStack()
        modw = sb("modw", [P, MS, KT, 256], F32, prs)
        rows = sb("rows", [2, 2, 256], F32, prs)
        s5p = sb("s5p", [P, 3, 64], F32, prs)
        sB = sb("sB", [P, 64, 2, C16], F32, prs)
        sC = sb("sC", [P, 64, 2, C16], F32, prs)
        sd = sb("sd", [P, KT], F32, prs)
        v = sb("v", [P, 24, 64], F32, prs)
        pw = sb("pw", [P, 2, 64, L + 1], F32, prs)
        cf = sb("cf", [P, 64, 2, C16], F32, prs)
        bz = sb("bz", [P, 8, 2, 2 * C16], F32, prs)
        et = sb("et", [P, 3, 32, NK], F32, prs)
        bx = sb("bx", [P, 8, 2, L, C16], F32, prs)
        cx = sb("cx", [P, 8, 2, L + 1, C16], F32, prs)
        t1 = sb("t1", [P, 64 * C16], F32, prs)
        t2 = sb("t2", [P, 64 * C16], F32, prs)
        t3 = sb("t3", [P, GPB * (L + 1) * C16], F32, prs)
        t4 = sb("t4", [P, GPB * (L + 1) * C16], F32, prs)
        vws = sb("vws", [P, 8, 2, P], F32, prs)
        zs = sb("zs", [P, ZW, C16], F32, prs)
        prs.close()

        vwd = nc.dram_tensor("vwd", (NB5, P, 8, 2, P), F32, kind="Internal").ap()
        cxd = nc.dram_tensor("cxd", (NB5, P, 8, 2, L + 1, C16), F32, kind="Internal").ap()
        etd = nc.dram_tensor("etd", (NB5, P, 3, 8, NK), F32, kind="Internal").ap()
        zd = nc.dram_tensor("zd", (D, ZW * C16), F32, kind="Internal").ap()
        hd = nc.dram_tensor("hd", (D, T), F32, kind="Internal").ap()
        yd = nc.dram_tensor("yd", (D, T), F32, kind="Internal").ap()

        s5st = ExitStack()
        U = sb("U", [P, G, NK], F32, s5st)
        hS = sb("hS", [P, KT, L, NK], F32, s5st)
        vwS = sb("vwS", [P, 2, 8, 2, P], F32, s5st)
        cxS = sb("cxS", [P, 2, 8, 2, L + 1, C16], F32, s5st)
        etS = sb("etS", [P, 2, 3, 8, NK], F32, s5st)
        mS = sb("mS", [P, 2, 8, P], F32, s5st)
        Yt = sb("Yt", [P, 2, 8, NK], F32, s5st)
        wr = sb("wr", [P, 2, 8 * NK], F32, s5st)
        gr = sb("gr", [P, 2, 8 * NK], F32, s5st)
        ta = sb("ta", [P, 8, NK], F32, s5st)
        tb = sb("tb", [P, 8, NK], F32, s5st)
        tc = sb("tc", [P, 8, NK], F32, s5st)
        td = sb("td", [P, 8, NK], F32, s5st)
        Hs = sb("Hs", [P, 2, 2, 8, NK + 1], F32, s5st)
        s5st.close()

        s5_par = sem("s5_par")
        v_step = sem("v_step")
        v_act = sem("v_act")
        et_ready = sem("et_ready")
        et_out = sem("et_out")
        bx_ready = sem("bx_ready")
        cx_ready = sem("cx_ready")
        cf_ready = sem("cf_ready")
        c_step = sem("c_step")
        bxT_ready = sem("bxT_ready")
        z_ready = sem("z_ready")
        vws_ready = sem("vws_ready")
        zs_ready = sem("zs_ready")
        vw_out = sem("vw_out")
        cx_out = sem("cx_out")
        z_out = sem("z_out")
        hd_out = pair("hd_out")
        u_in = pair("u_in")
        v5_in = pair("v5_in")
        e5_in = pair("e5_in")
        y5_in = pair("y5_in")
        V_ready = sem("V_ready")
        V_used = sem("V_used")
        r_step = sem("r_step")
        g_ready = sem("g_ready")
        q_step = sem("q_step")
        H_zero = sem("H_zero")
        H_ready = sem("H_ready")
        Y_ready = sem("Y_ready")
        Yt_ready = sem("Yt_ready")
        y_out = pair("y_out")
        y_in = pair("y_in")
        gelu_ready = sem("gelu_ready")
        zh_ready = sem("zh_ready")
        zl_ready = sem("zl_ready")
        sig_ready = pair("sig_ready")
        glu_ready = pair("glu_ready")
        glu_free = pair("glu_free")
        (DT, ER, ANG, RN, RR, SH, SN, CS, MAG, M8, AR, AI, NRE, DEN, FR, FI, E2R, E2I, E4R, E4I, E8R, E8I, VA, VB) = range(24)

        def col(i):
            return v[:, i, :]

        def prep_act(act):
            act.wait_ge(s5_par, 16 * 5)
            act.activation(col(DT), s5p[:, 2, :], ACT.Exp).then_inc(v_act, 1)
            act.wait_ge(v_step, 1)
            act.activation(col(MAG), col(ER), ACT.Exp).then_inc(v_act, 1)
            act.activation(col(M8), col(ER), ACT.Exp, scale=float(L)).then_inc(v_act, 1)
            act.wait_ge(v_step, PREP_ANGLE)
            act.activation(col(SN), col(RR), ACT.Sin).then_inc(v_act, 1)
            act.activation(col(SH), col(RR), ACT.Sin, scale=0.5).then_inc(v_act, 1)
            mods_act(act, 0, MHEAD)
            for b in range(NB5):
                if b:
                    act.wait_ge(vw_out, 16 * b)
                for q in range(4):
                    act.wait_ge(bxT_ready, 4 * b + q + 1)
                    act.activation(vws[:, 2 * q:2 * q + 2, :, :].rearrange("p a b c -> p (a b c)"), PS[:, q, :], ACT.Copy)\
                        .then_inc(vws_ready, 1)
                if MHEAD + b < MB // MU:
                    mods_act(act, MHEAD + b, MHEAD + b + 1)

        def prep_dve(dve):
            done = [0]

            def step(ins):
                done[0] += 1
                ins.then_inc(v_step, 1)
                dve.wait_ge(v_step, done[0])

            def tt(dst, a, b, op):
                step(dve.tensor_tensor(dst, a, b, op))

            def cmul(dr, di, ar, ai, br, bi, ta_, tb_, negative=False):
                tt(ta_, ar, br, ALU.mult)
                tt(tb_, ai, bi, ALU.mult)
                tt(dr, ta_, tb_, ALU.subtract)
                tt(ta_, ar, bi, ALU.mult)
                tt(tb_, ai, br, ALU.mult)
                if negative:
                    step(dve.scalar_tensor_tensor(out=di, in0=ta_, scalar=-1.0, in1=tb_, op0=ALU.mult, op1=ALU.subtract))
                else:
                    tt(di, ta_, tb_, ALU.add)

            are, aim = s5p[:, 0, :], s5p[:, 1, :]
            dve.wait_ge(s5_par, 16 * 5)
            dve.wait_ge(v_act, 1)
            tt(col(ER), are, col(DT), ALU.mult)
            tt(col(ANG), aim, col(DT), ALU.mult)
            magic = 1.5 * 2.0 ** 23
            step(dve.tensor_scalar(col(RN), col(ANG), 1.0 / (2.0 * np.pi), magic, ALU.mult, ALU.add))
            step(dve.tensor_scalar(col(RN), col(RN), magic, None, ALU.subtract))
            step(dve.scalar_tensor_tensor(out=col(RR), in0=col(RN), scalar=-TWO_PI[0], in1=col(ANG), op0=ALU.mult, op1=ALU.add))
            step(dve.scalar_tensor_tensor(out=col(RR), in0=col(RN), scalar=-TWO_PI[1], in1=col(RR), op0=ALU.mult, op1=ALU.add))
            step(dve.scalar_tensor_tensor(out=col(RR), in0=col(RN), scalar=-TWO_PI[2], in1=col(RR), op0=ALU.mult, op1=ALU.add))
            step(dve.tensor_scalar(col(RR), col(RR), 3.1415925, -3.1415925, ALU.min, ALU.max))
            assert done[0] == PREP_ANGLE
            dve.wait_ge(v_act, 5)
            tt(col(CS), col(SH), col(SH), ALU.mult)
            step(dve.tensor_scalar(col(CS), col(CS), -2.0, 1.0, ALU.mult, ALU.add))
            tt(col(AR), col(MAG), col(CS), ALU.mult)
            tt(col(AI), col(MAG), col(SN), ALU.mult)
            step(dve.tensor_scalar(col(NRE), col(AR), 1.0, None, ALU.subtract))
            tt(col(VA), are, are, ALU.mult)
            tt(col(VB), aim, aim, ALU.mult)
            tt(col(DEN), col(VA), col(VB), ALU.add)
            step(dve.reciprocal(col(DEN), col(DEN)))
            tt(col(VA), col(NRE), are, ALU.mult)
            tt(col(VB), col(AI), aim, ALU.mult)
            tt(col(FR), col(VA), col(VB), ALU.add)
            tt(col(FR), col(FR), col(DEN), ALU.mult)
            tt(col(VA), col(AI), are, ALU.mult)
            tt(col(VB), col(NRE), aim, ALU.mult)
            tt(col(FI), col(VA), col(VB), ALU.subtract)
            tt(col(FI), col(FI), col(DEN), ALU.mult)
            step(dve.memset(pw[:, 0, :, 0:1], 1.0))
            step(dve.memset(pw[:, 1, :, 0:1], 0.0))
            for r, c in ((0, AR), (1, AI)):
                step(dve.tensor_copy(pw[:, r, :, 1:2], col(c).unsqueeze(2)))
            for n in (1, 2, 4):
                by = [pw[:, r, :, n:n + 1].to_broadcast([P, 64, n]) for r in range(2)]
                ts = [t[:, 0:64 * n].rearrange("p (a b) -> p a b", b=n) for t in (t1, t2)]
                cmul(pw[:, 0, :, n + 1:2 * n + 1], pw[:, 1, :, n + 1:2 * n + 1],
                     pw[:, 0, :, 1:n + 1], pw[:, 1, :, 1:n + 1], by[0], by[1], ts[0], ts[1])
            cmul(col(E2R), col(E2I), col(CS), col(SN), col(CS), col(SN), col(VA), col(VB))
            cmul(col(E4R), col(E4I), col(E2R), col(E2I), col(E2R), col(E2I), col(VA), col(VB))
            cmul(col(E8R), col(E8I), col(E4R), col(E4I), col(E4R), col(E4I), col(VA), col(VB))
            for half in range(2):
                of_half = slice(32 * half, 32 * half + 32)
                if half:
                    dve.wait_ge(et_out, 16)
                step(dve.memset(et[:, 0, :, 0:1], 1.0))
                step(dve.memset(et[:, 1, :, 0:1], 0.0))
                n, cr, ci, nr, ni = 1, E8R, E8I, E2R, E2I
                while n < NK:
                    by = [col(c)[:, of_half].unsqueeze(2).to_broadcast([P, 32, n]) for c in (cr, ci)]
                    ts = [t[:, 0:32 * n].rearrange("p (a b) -> p a b", b=n) for t in (t1, t2)]
                    cmul(et[:, 0, :, n:2 * n], et[:, 1, :, n:2 * n], et[:, 0, :, 0:n], et[:, 1, :, 0:n], by[0], by[1], ts[0], ts[1])
                    if 2 * n < NK:
                        cmul(col(nr), col(ni), col(cr), col(ci), col(cr), col(ci), col(VA), col(VB))
                    n, cr, ci, nr, ni = 2 * n, nr, ni, *((E4R, E4I) if nr == E2R else (E2R, E2I))
                step(dve.tensor_copy(et[:, 2, :, :], col(M8)[:, of_half].unsqueeze(2).to_broadcast([P, 32, NK])))
                step(dve.memset(et[:, 2, :, 0:1], 0.0))
                dve.sem_inc(et_ready, 1)
            fb = [col(c).unsqueeze(2).to_broadcast([P, 64, C16]) for c in (FR, FI)]
            ts = [t[:, 0:64 * C16].rearrange("p (a b) -> p a b", b=C16) for t in (t1, t2)]
            cmul(cf[:, :, 0, :], cf[:, :, 1, :], sC[:, :, 0, :], sC[:, :, 1, :], fb[0], fb[1], ts[0], ts[1])
            dve.sem_inc(cf_ready, 1)
            step(dve.memset(bz[:, :, :, :], 0.0))
            for b in range(NB5):
                if b:
                    dve.wait_ge(bxT_ready, 4 * b)
                    dve.wait_ge(z_ready, b)
                for g2 in range(2):
                    step(dve.tensor_copy(bz[64 * g2:64 * g2 + 64, :, :, C16 * g2:C16 * g2 + C16],
                                         sB[64 * g2:64 * g2 + 64, 8 * b:8 * b + 8, :, :]))
                for d in range(2):
                    ts = [t[:, 0:GPB * P].rearrange("p (a b c) -> p a b c", a=GPB, b=L) for t in (t1, t2)]
                    back, lo = ((True, 1), (False, 0))[d]
                    cmul(bx[:, d::2, 0, :, :], bx[:, d::2, 1, :, :], channels(sB, b, 0, d, L), channels(sB, b, 1, d, L),
                         powers(b, 0, d, lo, lo + L, back), powers(b, 1, d, lo, lo + L, back), ts[0], ts[1])
                dve.sem_inc(bx_ready, 1)
                dve.wait_ge(z_ready, b + 1)
                if b:
                    dve.wait_ge(z_out, 16 * b)
                step(dve.tensor_copy(zs[:, :, :], PS[:, 7, 0:ZW * C16].rearrange("p (a b) -> p a b", b=C16)))
                step(dve.scalar_tensor_tensor(out=zs[:, L - 1, :], in0=const("m16")[:, 0:C16], scalar=sd[:, b:b + 1],
                                              in1=zs[:, L - 1, :], op0=ALU.mult, op1=ALU.add))
                dve.sem_inc(zs_ready, 1)

        def powers(b, r, d, lo, hi, back):
            t = pw[:, r, 8 * b + d:8 * b + 8:2, :]
            if back:
                t = t[:, :, ::-1]
            return t[:, :, lo:hi].unsqueeze(3).to_broadcast([P, GPB, hi - lo, C16])

        def channels(t, b, r, d, n):
            return t[:, 8 * b + d:8 * b + 8:2, r, :].unsqueeze(2).to_broadcast([P, GPB, n, C16])

        def prep_pool(pool):
            n = [0]

            def step(ins):
                n[0] += 1
                ins.then_inc(c_step, 1)
                pool.wait_ge(c_step, n[0])

            for half in range(2):
                pool.wait_ge(et_ready, half + 1)
                pool.dma_start(etd[4 * half:4 * half + 4].rearrange("b p r g k -> p r b (g k)"),
                               et[:, :, :, :].rearrange("p r (b g) k -> p r b (g k)", b=4)).then_inc(et_out, 16)
            pool.wait_ge(cf_ready, 1)
            for b in range(NB5):
                if b:
                    pool.wait_ge(cx_out, 16 * b)
                    pool.wait_ge(z_ready, b)
                for d in range(2):
                    ta_, tb_ = (t[:, :].rearrange("p (a b c) -> p a b c", a=GPB, b=L + 1) for t in (t3, t4))
                    cr, ci = channels(cf, b, 0, d, L + 1), channels(cf, b, 1, d, L + 1)
                    pr, pi = powers(b, 0, d, 0, L + 1, d == 1), powers(b, 1, d, 0, L + 1, d == 1)
                    step(pool.tensor_tensor(ta_, cr, pr, ALU.mult))
                    step(pool.tensor_tensor(tb_, ci, pi, ALU.mult))
                    step(pool.tensor_tensor(cx[:, d::2, 0, :, :], ta_, tb_, ALU.subtract))
                    step(pool.tensor_tensor(ta_, cr, pi, ALU.mult))
                    step(pool.tensor_tensor(tb_, ci, pr, ALU.mult))
                    step(pool.tensor_tensor(ta_, ta_, tb_, ALU.add))
                    step(pool.tensor_scalar(cx[:, d::2, 1, :, :], ta_, -1.0, None, ALU.mult))
                pool.sem_inc(cx_ready, 1)
                pool.dma_start(cxd[b], cx[:, :, :, :, :]).then_inc(cx_out, 16)
                pool.wait_ge(vws_ready, 4 * b + 4)
                pool.dma_start(vwd[b], vws[:, :, :, :]).then_inc(vw_out, 16)
                pool.wait_ge(zs_ready, b + 1)
                pool.dma_start(zd[b * P:(b + 1) * P, :], zs[:, :, :].rearrange("p a b -> p (a b)")).then_inc(z_out, 16)

        def prep_pe(pe):
            pe.wait_ge(c_in, 32)
            mods_pe(pe, 0, MHEAD)
            for b in range(NB5):
                pe.wait_ge(bx_ready, b + 1)
                for q in range(4):
                    if b:
                        pe.wait_ge(vws_ready, 4 * (b - 1) + q + 1)
                    for j in range(4):
                        last = pe.transpose(PS[:, q, j * P:(j + 1) * P],
                                            bx[:, 2 * q + j // 2, j % 2, :, :].rearrange("p a b -> p (a b)"), const("eye"))
                    last.then_inc(bxT_ready, 1)
                pe.wait_ge(cx_ready, b + 1)
                if b:
                    pe.wait_ge(zs_ready, b)
                for pr in range(GPB):
                    for d in range(2):
                        for r in range(2):
                            gd = 2 * pr + d
                            lag = cx[:, gd, r, d:d + L, :].rearrange("p a b -> p (a b)")
                            at = (0 if d else (L - 1) * C16)
                            last = pe.matmul(PS[32 * pr:32 * pr + 32, 7, at:at + P], bz[:, gd, r, :], lag,
                                             start=d == 0 and r == 0, stop=True, skip_group_check=True,
                                             tile_position=(0, 32 * pr))
                last.then_inc(z_ready, 1)
                if MHEAD + b < MB // MU:
                    mods_pe(pe, MHEAD + b, MHEAD + b + 1)

        def load_v(sp, b):
            sp.dma_start(vwS[:, b % 2, :, :, :], vwd[b]).then_inc(v5_in[b % 2], 16)

        def load_e(sp, b):
            sp.dma_start(etS[:, b % 2, :, :, :], etd[b]).then_inc(e5_in[b % 2], 16)

        def load_y(sp, b):
            sp.dma_start(cxS[:, b % 2, :, :, :, :], cxd[b]).then_inc(y5_in[b % 2], 16)
            for st in range(L):
                src = bass.AP(zd.tensor, zd.offset + b * P * ZW * C16 + (L - 1 - st) * C16,
                              [[ZW * C16, C16], [C16 * ZW * C16, 8], [1, P]])
                sp.dma_start(mS[C16 * st:C16 * st + C16, b % 2, :, :], src).then_inc(y5_in[b % 2], 16)

        def back(eng, b):
            eng.wait_ge(y_out[b % 2], 16 * L * (b // 2 + 1))
            eng.dma_start(hS[:, b, :, :], yd[b * P:(b + 1) * P, :].rearrange("p (s k) -> p s k", s=L)).then_inc(y_in[b % 2], 16)

        def s5_sp(sp):
            for s_, n in ((et_out, 2), (cx_out, NB5), (vw_out, NB5), (z_out, NB5)):
                sp.wait_ge(s_, 16 * n)
            for q in range(2):
                sp.wait_ge(x_ready[q], 1 + KT // 2)
            load_v(sp, 0)
            for part_, (k0, k1) in enumerate(S5_PARTS):
                sp.wait_ge(hh_ready, pieces_before(1) + 2 * k1)
                sp.dma_start(hd.rearrange("(k p) t -> p k t", p=P)[:, k0:k1, :],
                             hS[:, k0:k1, :, :].rearrange("p k s c -> p k (s c)")).then_inc(hd_out[part_], 16)
                load_e(sp, part_)
                sp.wait_ge(hd_out[part_], 16)
                for st in range(L):
                    src = bass.AP(hd.tensor, hd.offset + k0 * P * T + st * NK, [[T, C16], [C16 * T, 8 * (k1 - k0)], [1, NK]])
                    sp.dma_start(U[C16 * st:C16 * st + C16, 8 * k0:8 * k1, :], src).then_inc(u_in[part_], 16)
                if part_ == 0:
                    load_v(sp, 1)
                load_y(sp, part_)
            for b in range(2, NB5):
                sp.wait_ge(V_ready, b - 1)
                load_v(sp, b)
                sp.wait_ge(H_ready, b - 1)
                load_e(sp, b)
                sp.wait_ge(Y_ready, b - 1)
                load_y(sp, b)
            sp.wait_ge(Yt_ready, NB5)
            back(sp, NB5 - 1)

        def scan_order(t, d):
            return t if d == 0 else t.rearrange("p (a j) -> p a j", a=2)[:, :, ::-1]

        def s5_pe(pe):
            for b in range(NB5 + 1):
                s = b % 2
                if b < NB5:
                    pe.wait_ge(v5_in[s], 16 * (b // 2 + 1))
                    pe.wait_ge(u_in[b >= S5_PARTS[0][1]], 16 * L)
                    if b >= 2:
                        pe.wait_ge(V_used, b - 1)
                    for gd in range(8):
                        for r in range(2):
                            for g2 in range(2):
                                g = 8 * b + 2 * (gd // 2) + g2
                                last = pe.matmul(PS[64 * g2:64 * g2 + 64, 2 * s + r, gd * NK:(gd + 1) * NK],
                                                 vwS[:, s, gd, r, 64 * g2:64 * g2 + 64], scan_order(U[:, g, :], gd % 2),
                                                 start=True, stop=True)
                    last.then_inc(V_ready, 1)
                if b:
                    c = b - 1
                    s = c % 2
                    pe.wait_ge(y5_in[s], 16 * (L + 1) * (c // 2 + 1))
                    pe.wait_ge(H_ready, c + 1)
                    if c >= 2:
                        pe.wait_ge(Yt_ready, c - 1)
                    for gl in range(8):
                        pr, g2 = gl // 2, gl % 2
                        rows = slice(64 * g2, 64 * g2 + 64)
                        dst = PS[:, 4 + 2 * s + g2, pr * NK:(pr + 1) * NK]
                        pe.matmul(dst, mS[:, s, gl, :], U[:, 8 * c + gl, :], start=True, stop=False)
                        for d in range(2):
                            for r in range(2):
                                w = cxS[rows, s, 2 * pr + d, r, 1 - d:1 - d + L, :].rearrange("p a b -> p (a b)")
                                last = pe.matmul(dst, w, scan_order(Hs[rows, s, r, 2 * pr + d, 0:NK], d),
                                                 start=False, stop=d == 1 and r == 1)
                    last.then_inc(Y_ready, 1)

        def s5_dve(dve):
            n = [0]

            def step(ins):
                n[0] += 1
                ins.then_inc(r_step, 1)
                dve.wait_ge(r_step, n[0])

            for b in range(NB5):
                s = b % 2
                dve.wait_ge(e5_in[s], 16 * (b // 2 + 1))
                dve.wait_ge(V_ready, b + 1)
                vr, vi = (PS[:, 2 * s + r, :].rearrange("p (g k) -> p g k", k=NK) for r in range(2))
                ec, es = etS[:, s, 0, :, :], etS[:, s, 1, :, :]
                mult = etS[:, s, 2, :, :].rearrange("p g k -> p (g k)")
                wre, wim = (wr[:, r, :].rearrange("p (g k) -> p g k", k=NK) for r in range(2))
                dve.tensor_tensor(ta[:, :, :], vr, ec, ALU.mult)
                step(dve.tensor_tensor(tb[:, :, :], vi, es, ALU.mult))
                step(dve.tensor_tensor(wre, ta[:, :, :], tb[:, :, :], ALU.add))
                dve.tensor_tensor(ta[:, :, :], vi, ec, ALU.mult)
                last = dve.tensor_tensor(tb[:, :, :], vr, es, ALU.mult)
                step(last)
                step(dve.tensor_tensor(wim, ta[:, :, :], tb[:, :, :], ALU.subtract))
                dve.sem_inc(V_used, 1)
                if b:
                    dve.wait_ge(q_step, 6 * b)
                for r in range(2):
                    last = dve.tensor_tensor_scan(gr[:, r, :], mult, wr[:, r, :], 0.0, ALU.mult, ALU.add)
                    last.then_inc(g_ready, 1)
            for k in range(KT):
                dve.wait_ge(zh_ready, k + 1)
                dve.tensor_tensor(hl[:, k, :], hS[:, k, :, :].rearrange("p s c -> p (s c)"), hh[:, k, :].bitcast(F32), ALU.subtract)\
                    .then_inc(zl_ready, 1)

            def glu(i, s):
                dt = 2 * i + s
                dve.wait_ge(sig_ready[s], i + 1)
                dve.scalar_tensor_tensor(out=gt[:, s, :], in0=PS[:, s, :], scalar=glub[:, 0, bass.ds(dt, 1)],
                                         in1=sil[:, s, :], op0=ALU.add, op1=ALU.mult).then_inc(glu_ready[s], 1)
                dve.wait_ge(glu_ready[s], 1 + i + 1)
                for w in range(2):
                    xv = x[:, bass.ds(dt, 1), cols(w)].rearrange("p a (k s) -> p (a s) k", s=L)
                    last = dve.scalar_tensor_tensor(
                        out=xv, in0=gt[:, s, :].rearrange("p (s k) -> p s k", s=L)[:, :, KC * w:KC * w + KC],
                        scalar=hg[:, 0, 1, bass.ds(dt, 1), w:w + 1].rearrange("p a b -> p (a b)"), in1=xv,
                        op0=ALU.mult, op1=ALU.add)
                last.then_inc(x_ready[s], 1)

            blocks(dve, "glu", split_lo, glu)

        def s5_pool(pool):
            m = 0
            pool.wait_ge(hh_ready, pieces_before(2))
            pool.memset(Hs[:, :, :, :, 0:1].rearrange("p a b c d -> p (a b c) d"), 0.0).then_inc(H_zero, 1)
            for b in range(NB5):
                s = b % 2
                pool.wait_ge(g_ready, 2 * b + 2)
                if b >= 2:
                    pool.wait_ge(Y_ready, b - 1)
                ec, es = etS[:, s, 0, :, :], etS[:, s, 1, :, :]
                gre, gim = (gr[:, r, :].rearrange("p (g k) -> p g k", k=NK) for r in range(2))
                hre, him = Hs[:, s, 0, :, 1:NK + 1], Hs[:, s, 1, :, 1:NK + 1]
                for a, c, e, f, dst, op in ((gre, ec, gim, es, hre, ALU.subtract), (gre, es, gim, ec, him, ALU.add)):
                    pool.tensor_tensor(tc[:, :, :], a, c, ALU.mult).then_inc(q_step, 1)
                    pool.tensor_tensor(td[:, :, :], e, f, ALU.mult).then_inc(q_step, 1)
                    m += 2
                    pool.wait_ge(q_step, m)
                    pool.tensor_tensor(dst, tc[:, :, :], td[:, :, :], op).then_inc(q_step, 1)
                    m += 1
                    pool.wait_ge(q_step, m)
                pool.sem_inc(H_ready, 1)

        def s5_act(act):
            def gelu(b):
                act.wait_ge(y_in[b % 2], 16 * (b // 2 + 1))
                act.activation(hS[:, b, :, :], hS[:, b, :, :], ACT.Gelu_apprx_tanh).then_inc(gelu_ready, 1)

            def high_part(k):
                act.wait_ge(gelu_ready, k + 1)
                act.activation(hh[:, k, :], hS[:, k, :, :].rearrange("p s c -> p (s c)"), ACT.Copy).then_inc(zh_ready, 1)

            for b in range(NB5):
                act.wait_ge(Y_ready, b + 1)
                if b >= 2:
                    act.wait_ge(y_out[b % 2], 16 * L * (b // 2))
                y = PS[:, 4 + 2 * (b % 2):6 + 2 * (b % 2), 0:GPB * NK].rearrange("p g (r k) -> p r g k", k=NK)
                act.activation(Yt[:, b % 2, :, :].rearrange("p (r g) k -> p r g k", g=2), y, ACT.Copy).then_inc(Yt_ready, 1)
                act.wait_ge(Yt_ready, b + 1)
                for st in range(L):
                    dst = bass.AP(yd.tensor, yd.offset + b * P * T + st * NK, [[T, C16], [C16 * T, 8], [1, NK]])
                    act.dma_start(dst, Yt[C16 * st:C16 * st + C16, b % 2, :, :]).then_inc(y_out[b % 2], 16)
                if b >= 1:
                    back(act, b - 1)
                if b >= 2:
                    gelu(b - 2)
            for k in range(KT - 2):
                high_part(k)
            gelu(NB5 - 2)
            high_part(KT - 2)
            gelu(NB5 - 1)
            high_part(KT - 1)

            def gate(i, s):
                act.wait_ge(blk_done[s], 1 + BASE["glu"] // 2 + i + 1)
                act.activation(sil[:, s, :], PS[:, 2 + s, :], ACT.Sigmoid, bias=glub[:, 1, bass.ds(2 * i + s, 1)]).then_inc(sig_ready[s], 1)

            blocks(act, "glu", split_hi, gate)

        def glu_pe(pe):
            with pe.Fori(0, KT // 2) as i:
                for s in range(2):
                    pe.wait_ge(wlo_ready[s], 1 + BASE["glu"] // 2 + i + 1)
                    pe.wait_ge(glu_ready[s], 1 + i)
                    for ab in range(2):
                        for k in range(KT):
                            if s == 0 and ab == 0:
                                pe.wait_ge(zl_ready, k + 1)
                            last = mm3(pe, PS[:, 2 * ab + s, :], s, (2 * k + ab) * P, hh[:, k, :], hl[:, k, :], k == 0, k == KT - 1)
                    last.then_inc(blk_done[s], 1)
        gst = ExitStack()
        pk = sb("pk", [P, 2, CTX + 4], F32, gst)
        pv = sb("pv", [P, 2, CTX + 4], F32, gst)
        pq = sb("pq", [P, 1, LAT + 4], F32, gst)
        ck = sb("ck", [P, 2, CTX], F32, gst)
        cv = sb("cv", [P, 2, CTX], F32, gst)
        cq = sb("cq", [P, 1, LAT], F32, gst)
        sqk, sqq = rstd, std[:, LAT:2 * LAT]
        kn = sb("kn", [P, NCH, CH], F32, gst)
        qn = sb("qn", [P, 2, CH], F32, gst)
        vt = sb("vt", [P, NCH, CH], F32, gst)
        kd = sb("kd", [P, 2, NCH, CH], F32, gst)
        zn = sb("zn", [P, LAT], F32, gst)
        zg = sb("zg", [P, LAT], F32, gst)
        zo = std[:, 0:LAT]
        DTm = sb("DTm", [P, 2, NCH, CH], F32, gst)
        DTs = sb("DTs", [P, 2, NCH, CH], F32, gst)
        DTi = sb("DTi", [P, 2, 2, CH], F32, gst)
        NT = sb("NT", [P, 2, NCH, CH], F32, gst)
        NN = sb("NN", [P, 2, NCH, CH], F32, gst)
        X = sb("X", [P, 2, NCH, CH], F32, gst)
        BT = sb("BT", [P, 2, NCH, CH], F32, gst)
        BB = sb("BB", [P, 2, NCH, CH], F32, gst)
        EE = sb("EE", [P, 2, 3, NCH, CH], F32, gst)
        at = sb("at", [P, 2, 2, CH], F32, gst)
        S = sb("S", [P, 2, CH], F32, gst)
        r2 = sb("r2", [P, 2, CH], F32, gst)
        vn = sb("vn", [P, 2, CH], F32, gst)
        o1 = sb("o1", [P, 2, CH], F32, gst)
        oo = sb("oo", [P, 2, 2, CH], F32, gst)
        on = sb("on", [P, 2, CH], F32, gst)
        yt = sb("yt", [P, LAT], F32, gst)
        vec = sb("vec", [P, 6, NCH, 2, H], F32, gst)
        hv = sb("hv", [P, 6, NCH, 2], F32, gst)
        gw = sb("gw", [P, 10, NCH, 2 * H], F32, gst)
        etv = sb("etv", [P, NCH, 2], F32, gst)
        oss = sb("oss", [P, 4], F32, gst)
        convw = sb("convw", [P, H, 3, 5], F32, gst)
        gpar = sb("gpar", [P, 2, 2 * H], F32, gst)
        gng = sb("gng", [P, 1], F32, gst)
        yh = sb("yh", [P, H + 1, LAT], F32R, gst)
        yl = sb("yl", [P, H + 1, LAT], F32R, gst)
        gst.close()
        BETA, NBETA, GG, GC, EG, EK = range(6)

        PER = {"hv": 1, "pc": 3, "zg": 1, "conv": 15, "silu": 3, "square": 2, "sumsq": 2, "root": 2, "recip": 2, "kn": 2,
               "kT": 1, "vT": 1, "vt": 1, "kd": 2, "gram": 2, "zc": 1, "zo": 1, "gcB": 2, "dmin": 2, "dexp": 2, "mask": 6, "nt": 2, "at": 2,
               "ntT": 2, "nn": 2, "b0": 4, "x0": 2, "ee": 2, "prod": 20, "eva": 12, "evd": 20, "RS": 6, "r2": 6, "TV": 8,
               "vn": 8, "KV": 8, "S": 6, "o1": 4, "oo": 4, "osum": 1, "oss": 2, "oroot": 1, "orec": 1, "on": 1, "oT": 1,
               "yt": 1, "yh": 1, "yl": 1}
        gs_ = {n: sem("g_" + n) for n in PER}
        gp_in = sem("gp_in")
        gstep = sem("gstep")
        gact = sem("gact")
        gate_mm = sem("gate_mm")
        zg_zero = sem("zg_zero")
        gate_done = sem("gate_done")
        gba_ready = sem("gba_ready")

        def need(eng, name, h, n):
            eng.wait_ge(gs_[name], PER[name] * h + n + (name in ("yt", "yl", "zc", "osum")))

        def told(ins, name):
            ins.then_inc(gs_[name], 1)

        ORDER = [(0, 1, 2, 3), (1, 0, 3, 2)]
        ACT_ROUNDS = [0, 1, 2, 4, 6, 8]

        def gates_pe(pe):
            pe.wait_ge(gba_ready, 2)
            for c in range(NCH):
                dst = PS[:, 7, 32 * c:32 * c + 32]
                for k in range(KT):
                    th, tl = hh[:, k, c * CH:(c + 1) * CH], hl[:, k, c * CH:(c + 1) * CH]
                    pe.matmul(dst, th, gwah[:, k, :], start=k == 0, stop=False)
                    pe.matmul(dst, tl, gwah[:, k, :], start=False, stop=False)
                    last = pe.matmul(dst, th, gwal[:, k, :], start=False, stop=k == KT - 1)
            last.then_inc(gate_mm, 1)
            pe.wait_ge(gstep, GATE_G)
            for c in range(NCH):
                for d in range(2):
                    at_ = 128 + 16 * c + 8 * d
                    pe.matmul(PS[:, 7, at_:at_ + 8], const(f"tri{d}"), vec[:, GG, c, d, :], start=True, stop=True)
                last = pe.matmul(PS[:, 7, 192 + 16 * c:208 + 16 * c], const("one"), vec[:, GG, c, :, :].rearrange("p a b -> p (a b)"),
                                 start=True, stop=True)
            last.then_inc(gate_mm, 1)

        def gates_act(act):
            raw_ba = PS[:, 7, 0:128].rearrange("p (c j) -> p c j", j=32)
            act.wait_ge(gp_in, 16 * 4)
            act.activation(gwah[:, :, :], gwa[:, :, :], ACT.Copy).then_inc(gba_ready, 1)
            act.wait_ge(gate_mm, 1)
            act.activation(vec[:, BETA, :, :, :].rearrange("p c d h -> p c (d h)"), raw_ba[:, :, 0:16], ACT.Sigmoid).then_inc(gact, 1)
            act.activation(gpar[:, 0, :], gpar[:, 0, :], ACT.Exp).then_inc(gact, 1)
            act.wait_ge(gstep, 2)
            act.activation(gw[:, 2, :, :], gw[:, 1, :, :], ACT.Exp).then_inc(gact, 1)
            act.wait_ge(gstep, 3)
            act.activation(gw[:, 4, :, :], gw[:, 3, :, :], ACT.Ln).then_inc(gact, 1)
            act.wait_ge(gstep, GATE_G + 3)
            act.activation(vec[:, EG, :, :, :].rearrange("p c d h -> p c (d h)"),
                           vec[:, GC, :, :, :].rearrange("p c d h -> p c (d h)"), ACT.Exp).then_inc(gact, 1)
            act.activation(vec[:, EK, :, :, :].rearrange("p c d h -> p c (d h)"), gw[:, 8, :, :], ACT.Exp).then_inc(gact, 1)
            act.activation(gw[:, 9, :, :], gw[:, 7, :, :], ACT.Exp).then_inc(gact, 1)

        def gates_dve(dve):
            n = [0]

            def step(ins):
                n[0] += 1
                ins.then_inc(gstep, 1)
                dve.wait_ge(gstep, n[0])

            raw_ba = PS[:, 7, 0:128].rearrange("p (c j) -> p c j", j=32)
            dtb = gpar[:, 1, :].unsqueeze(1).to_broadcast([P, NCH, 2 * H])
            ea = gpar[:, 0, :].unsqueeze(1).to_broadcast([P, NCH, 2 * H])
            dve.wait_ge(gba_ready, 1)
            dve.tensor_tensor(gwal[:, :, :], gwa[:, :, :], gwah[:, :, :].bitcast(F32), ALU.subtract).then_inc(gba_ready, 1)
            dve.wait_ge(gact, 1)
            a, na, e, u, ln, q, w, tot, rest = (gw[:, i, :, :] for i in range(9))
            step(dve.tensor_tensor(a, raw_ba[:, :, 16:32], dtb, ALU.add))
            step(dve.scalar_tensor_tensor(out=na, in0=a, scalar=-1.0, in1=a, op0=ALU.mult, op1=ALU.min))
            dve.wait_ge(gact, 3)
            step(dve.tensor_scalar(u, e, 1.0, None, ALU.add))
            step(dve.tensor_scalar(q, u, -1.0, None, ALU.add))
            step(dve.tensor_tensor(q, e, q, ALU.subtract))
            step(dve.reciprocal(w, u))
            step(dve.tensor_tensor(q, q, w, ALU.mult))
            dve.wait_ge(gact, 4)
            step(dve.tensor_tensor(q, q, ln, ALU.add))
            step(dve.scalar_tensor_tensor(out=q, in0=a, scalar=0.0, in1=q, op0=ALU.max, op1=ALU.add))
            g = vec[:, GG, :, :, :].rearrange("p c d h -> p c (d h)")
            step(dve.scalar_tensor_tensor(out=g, in0=q, scalar=-1.0, in1=ea, op0=ALU.mult, op1=ALU.mult))
            assert n[0] == GATE_G
            dve.wait_ge(gate_mm, 2)
            gc = vec[:, GC, :, :, :].rearrange("p c d h -> p c (d h)")
            step(dve.tensor_copy(gc, PS[:, 7, 128:192].rearrange("p (c j) -> p c j", j=16)))
            step(dve.tensor_copy(tot, PS[:, 7, 192:256].rearrange("p (c j) -> p c j", j=16)))
            step(dve.tensor_tensor(rest, tot, gc, ALU.subtract))
            step(dve.tensor_scalar(vec[:, NBETA, :, :, :].rearrange("p c d h -> p c (d h)"),
                                   vec[:, BETA, :, :, :].rearrange("p c d h -> p c (d h)"), -1.0, None, ALU.mult))
            dve.wait_ge(gact, 7)
            dve.sem_inc(gate_done, 1)

        def half_columns(t, d, level):
            return t.rearrange("p (b two j) -> p b two j", two=2, j=16 << level)[:, :, 1 - d, :]

        def project_pe(pe, h, meets_norm=False):
            for s, c0 in ((0, 0), (1, CTX)):
                pe.wait_ge(wlo_ready[s], 1 + BASE["gdn"] // 2 + h + 1)
                for ab in range(2):
                    for k in range(KT):
                        if meets_norm and s == 0 and ab == 0:
                            pe.wait_ge(norm_done, pieces_before(4, ("ffn", "gdn")) + 2 * (k + 1))
                        last = mm3(pe, PS[:, 2 * s + ab, 0:T - c0], s, (2 * k + ab) * P, hh[:, k, c0:T], hl[:, k, c0:T],
                                   k == 0, k == KT - 1)
                last.then_inc(blk_done[s], 1)

        def gdn_pe(pe):
            project_pe(pe, 0, meets_norm=True)
            gates_pe(pe)
            pe.wait_ge(gate_done, 1)

            def turn_output(h):
                need(pe, "on", h, 1)
                for c in range(2):
                    last = pe.transpose(PS[:, 0, c * CH:(c + 1) * CH], on[:, c, :], const("eye"))
                told(last, "oT")

            def head(h, ends):
                pe.wait_ge(gs_["osum"], 1 + h)
                need(pe, "square", h, 1)
                told(pe.matmul(PS[:, 4, :], const("one"), sqk[:, :], start=True, stop=True), "sumsq")
                need(pe, "square", h, 2)
                told(pe.matmul(PS[:, 5, 0:LAT], const("one"), sqq[:, :], start=True, stop=True), "sumsq")
                need(pe, "hv", h, 1)
                for d in range(2):
                    for c in range(NCH):
                        last = pe.matmul(PS[:, 6 + d, c * CH:(c + 1) * CH], hv[:, GG, c, d:d + 1].to_broadcast([P, CH]),
                                         const(f"tri{d}"), start=True, stop=True)
                    told(last, "gcB")
                if not ends:
                    need(pe, "pc", h, 3)
                    need(pe, "zg", h, 1)
                    project_pe(pe, h + 1)
                need(pe, "kn", h, 1)
                for c in range(NCH):
                    last = pe.transpose(PS[:, 4, c * CH:(c + 1) * CH], kn[:, c, :], const("eye"))
                told(last, "kT")
                if not ends:
                    need(pe, "pc", h + 1, 1)
                for c in range(NCH):
                    last = pe.matmul(PS[:, 0, c * CH:(c + 1) * CH], kn[:, c, :], kn[:, c, :], start=True, stop=True)
                told(last, "gram")
                need(pe, "kn", h, 2)
                need(pe, "silu", h, 2)
                vf = cv[:, :, :].rearrange("p a t -> p (a t)")
                for c in range(NCH):
                    last = pe.transpose(PS[:, 5, c * CH:(c + 1) * CH], vf[:, c * CH:(c + 1) * CH], const("eye"))
                told(last, "vT")
                if not ends:
                    need(pe, "pc", h + 1, 3)
                for c in range(2):
                    last = pe.matmul(PS[:, 2, c * CH:(c + 1) * CH], kn[:, 2 + c, :], qn[:, c, :], start=True, stop=True)
                told(last, "gram")
                for d in range(2):
                    need(pe, "nt", h, d + 1)
                    for c in range(NCH):
                        last = pe.transpose(PS[:, 6 + d, c * CH:(c + 1) * CH], NT[:, d, c, :], const("eye"))
                    told(last, "ntT")
                turn_output(h)
                if not ends:
                    need(pe, "zg", h + 1, 1)
                need(pe, "vt", h, 1)
                need(pe, "kd", h, 2)
                for rnd in range(10):
                    for d in range(2):
                        banks = ((1, 3, 6), (4, 5, 7))[d]
                        if rnd == 0:
                            need(pe, "b0", h, 2 * d + 2)
                            need(pe, "nn", h, d + 1)
                            need(pe, "x0", h, d + 1)
                        else:
                            need(pe, "evd", h, 2 * (rnd - 1) + d + 1)
                            if rnd - 1 in ACT_ROUNDS:
                                need(pe, "eva", h, 2 * ACT_ROUNDS.index(rnd - 1) + d + 1)
                            if rnd == 4:
                                need(pe, "ee", h, d + 1)
                        todo = [[(BB, BT), (BT, BB)], [(BB, X), (BB, BT), (BT, BB)], [(BB, X), (BT, BB)], [(BB, X)]]
                        level = (rnd - 4) // 2
                        if rnd < 4:
                            for (lt, rt), bank in zip(todo[rnd], banks):
                                for c in range(NCH):
                                    last = pe.matmul(PS[:, bank, c * CH:(c + 1) * CH], lt[:, d, c, :], rt[:, d, c, :], start=True, stop=True)
                        elif rnd % 2 == 0:
                            for c in range(NCH):
                                pe.transpose(PS[:, banks[0], c * CH:(c + 1) * CH], X[:, d, c, :], const("eye"))
                            for c in range(NCH):
                                last = pe.matmul(PS[:, banks[1], c * 64:(c + 1) * 64], EE[:, d, level, c, :],
                                                 half_columns(X[:, d, c, :], d, level), start=True, stop=True)
                        else:
                            for c in range(NCH):
                                last = pe.matmul(PS[:, banks[2], c * 64:(c + 1) * 64], BT[:, d, c, :],
                                                 BB[:, d, 0:2, :].rearrange("p a t -> p (a t)")[:, c * 64:(c + 1) * 64], start=True, stop=True)
                        told(last, "prod")
                for j in range(NCH):
                    for d in range(2):
                        c = ORDER[d][j]
                        if j:
                            need(pe, "S", h, 2 * (j - 1) + d + 1)
                            last = pe.matmul(PS[:, (1, 4)[d], 0:CH], kn[:, c, :], S[:, d, :], start=True, stop=True)
                            if c >= 2:
                                if j == 3:
                                    need(pe, "o1", h, d + 1)
                                last = pe.matmul(PS[:, 6 + d, 0:CH], qn[:, c - 2, :], S[:, d, :], start=True, stop=True)
                            told(last, "RS")
                    for d in range(2):
                        c = ORDER[d][j]
                        if j:
                            need(pe, "r2", h, 2 * (j - 1) + d + 1)
                            rhs = r2[:, d, :]
                        else:
                            need(pe, "evd", h, 19 + d)
                            rhs = vt[:, c, :]
                        told(pe.matmul(PS[:, (3, 5)[d], 0:CH], X[:, d, c, :], rhs, start=True, stop=True), "TV")
                    for d in range(2):
                        c = ORDER[d][j]
                        need(pe, "vn", h, 2 * j + d + 1)
                        if j == 0 and d == 0:
                            need(pe, "yt", h, 1)
                        if c >= 2:
                            last = pe.matmul(PS[:, (0, 2)[d], CH:2 * CH], at[:, d, c - 2, :], vn[:, d, :], start=True, stop=True)
                        if j < NCH - 1:
                            last = pe.matmul(PS[:, (0, 2)[d], 0:CH], kd[:, d, c, :], vn[:, d, :], start=True, stop=True)
                        told(last, "KV")
            with pe.Fori(0, H - 1) as h:
                head(h, False)
            head(H - 1, True)
            pe.wait_ge(gs_["osum"], 1 + H)
            turn_output(H)
            need(pe, "yl", H, 1)
            with pe.Fori(0, COUNT["wo"] // 2) as i:
                for s in range(2):
                    pe.wait_ge(wlo_ready[s], 1 + BASE["wo"] // 2 + i + 1)
                    for ab in range(2):
                        pe.wait_ge(x_ready[ab], 1 + KT // 2 * 4 + 2 * i + s - 1)
                        for k in range(KT):
                            last = mm3(pe, PS[:, 2 * ab + s, 0:LAT], s, (2 * k + ab) * P, yh[:, 1 + k, :], yl[:, 1 + k, :], k == 0, k == KT - 1)
                    last.then_inc(blk_done[s], 1)

        def gdn_act(act):
            u0 = BASE["gdn"] // 2

            def take(h):
                act.wait_ge(blk_done[0], 1 + u0 + h + 1)
                for bank, t in ((0, pk), (1, pv)):
                    told(act.activation(t[:, :, 2:CTX + 2], PS[:, bank, :].rearrange("p (a t) -> p a t", a=2), ACT.Copy), "pc")
                act.wait_ge(blk_done[1], 1 + u0 + h + 1)
                told(act.activation(pq[:, :, 2:LAT + 2], PS[:, 2:3, 0:LAT], ACT.Copy), "pc")
                act.wait_ge(gs_["zc"], 1 + h)
                told(act.activation(zn[:, :], PS[:, 3, 0:LAT], ACT.Silu), "zg")

            def shape(h):
                for j, t in enumerate((ck, cv, cq)):
                    need(act, "conv", h, 5 * j + 5)
                    told(act.activation(t[:, :, :], t[:, :, :], ACT.Silu), "silu")
                need(act, "silu", h, 1)
                told(act.activation(sqk[:, :], ck[:, :, :].rearrange("p a t -> p (a t)"), ACT.Square), "square")
                need(act, "silu", h, 3)
                told(act.activation(sqq[:, :], cq[:, 0, :], ACT.Square), "square")

            split_hi(act, 1, u0)
            split_hi(act, 0, u0 + 1)
            take(0)
            gates_act(act)
            shape(0)

            def output_squares(h):
                act.wait_ge(gs_["osum"], 1 + h)
                for c in range(2):
                    told(act.activation(on[:, c, :], oo[:, 0, c, :], ACT.Square, accum_out=oss[:, c:c + 1]), "oss")

            def output_root(h):
                need(act, "oss", h, 2)
                told(act.activation(oss[:, 2:4], oss[:, 0:2], ACT.Sqrt, scale=1.0 / CH, bias=epst[:, 0:1]), "oroot")

            def head(h, ends):
                output_squares(h)
                if not ends:
                    split_hi(act, 1, u0 + h + 1)
                need(act, "sumsq", h, 1)
                told(act.activation(sqk[:, :], PS[:, 4, :], ACT.Sqrt, bias=epst[:, 0:1]), "root")
                need(act, "sumsq", h, 2)
                told(act.activation(sqq[:, :], PS[:, 5, 0:LAT], ACT.Sqrt, bias=epst[:, 0:1]), "root")
                output_root(h)
                for d in range(2):
                    need(act, "dmin", h, d + 1)
                    told(act.activation(DTm[:, d, :, :], DTm[:, d, :, :], ACT.Exp), "dexp")
                if not ends:
                    split_hi(act, 0, u0 + h + 2)
                    take(h + 1)
                need(act, "vT", h, 1)
                told(act.activation(vt[:, :, :].rearrange("p c t -> p (c t)"), PS[:, 5, :], ACT.Copy), "vt")
                for d in range(2):
                    need(act, "ntT", h, d + 1)
                    told(act.activation(NN[:, d, :, :].rearrange("p c t -> p (c t)"), PS[:, 6 + d, :], ACT.Copy), "nn")
                for n, rnd in enumerate(ACT_ROUNDS):
                    for d in range(2):
                        banks = ((1, 3, 6), (4, 5, 7))[d]
                        need(act, "prod", h, 2 * rnd + d + 1)
                        copies = {0: [(BT, 0)], 1: [(BT, 1), (BB, 2)], 2: [(BB, 1)]}.get(rnd, [(BT, 0)])
                        for t, b in copies:
                            last = act.activation(t[:, d, :, :].rearrange("p c t -> p (c t)"), PS[:, banks[b], :], ACT.Copy)
                        told(last, "eva")
                if not ends:
                    shape(h + 1)
                for j in range(2, NCH):
                    for d in range(2):
                        c = ORDER[d][j]
                        need(act, "RS", h, 2 * (j - 1) + d + 1)
                        if j == 3:
                            need(act, "oo", h, d + 1)
                        told(act.activation(o1[:, d, :], PS[:, 6 + d, 0:CH], ACT.Copy, scale=hv[:, EG, c, d:d + 1]), "o1")
            with act.Fori(0, H - 1) as h:
                head(h, False)
            head(H - 1, True)
            output_squares(H)
            output_root(H)
            blocks(act, "wo", split_hi, lambda i, s: None)

        def gdn_dve(dve):
            u0 = BASE["gdn"] // 2

            def conv_steps(h):
                for n, (src, dst, which) in enumerate(((pk, ck, 1), (pv, cv, 2), (pq, cq, 0))):
                    for tap in range(5):
                        yield n, tap, src, dst, convw[:, bass.ds(h, 1), which, tap:tap + 1].rearrange("p a b -> p (a b)")

            def conv(h, n, tap, src, dst, w):
                win = src[:, :, tap:tap + CTX]
                if tap == 0:
                    need(dve, "pc", h, n + 1)
                    told(dve.tensor_scalar(dst[:, :, :], win, w, None, ALU.mult), "conv")
                else:
                    need(dve, "conv", h, 5 * n + tap)
                    told(dve.scalar_tensor_tensor(out=dst[:, :, :], in0=win, scalar=w, in1=dst[:, :, :], op0=ALU.mult, op1=ALU.add), "conv")

            split_lo(dve, 1, u0)
            split_lo(dve, 0, u0 + 1)
            for t in (pk, pv, pq):
                dve.memset(t[:, :, 0:2], 0.0)
                dve.memset(t[:, :, CTX + 2:CTX + 4], 0.0)
            dve.memset(zg[:, :], 0.0).then_inc(zg_zero, 1)
            dve.memset(oo[:, :, :, :], 0.0).then_inc(gs_["osum"], 1)
            gates_dve(dve)
            for one in conv_steps(0):
                conv(0, *one)

            def output_scaled(h):
                need(dve, "oroot", h, 1)
                told(dve.reciprocal(oss[:, 0:2], oss[:, 2:4]), "orec")
                need(dve, "orec", h, 1)
                for c in range(2):
                    last = dve.tensor_scalar(on[:, c, :], oo[:, 0, c, :], oss[:, c:c + 1], None, ALU.mult)
                told(last, "on")

            def output_gated(h):
                need(dve, "oT", h, 1)
                need(dve, "zo", h, 1)
                dve.wait_ge(gs_["yl"], 1 + h)
                told(dve.scalar_tensor_tensor(out=yt[:, :], in0=PS[:, 0, 0:LAT], scalar=gng[:, 0:1], in1=zo[:, :],
                                              op0=ALU.mult, op1=ALU.mult), "yt")

            def head(h, ends):
                dve.tensor_copy(hv[:, :, :, :].rearrange("p a c d -> p (a c d)").unsqueeze(2),
                                vec[:, :, :, :, bass.ds(h, 1)].rearrange("p a c d h -> p (a c d) h"))
                told(dve.tensor_copy(etv[:, :, :].rearrange("p c d -> p (c d)").unsqueeze(2),
                                     gw[:, 9, :, :].rearrange("p c (d h) -> p (c d) h", h=H)[:, :, bass.ds(h, 1)]), "hv")
                need(dve, "hv", h, 1)
                if not ends:
                    split_lo(dve, 1, u0 + h + 1)
                need(dve, "root", h, 1)
                told(dve.reciprocal(sqk[:, :], sqk[:, :]), "recip")
                need(dve, "recip", h, 1)
                told(dve.tensor_tensor(kn[:, :, :].rearrange("p c t -> p (c t)"), ck[:, :, :].rearrange("p a t -> p (a t)"), sqk[:, :], ALU.mult),
                     "kn")
                need(dve, "root", h, 2)
                told(dve.reciprocal(sqq[:, :], sqq[:, :]), "recip")
                need(dve, "recip", h, 2)
                told(dve.scalar_tensor_tensor(out=qn[:, :, :].rearrange("p c t -> p (c t)"), in0=cq[:, 0, :], scalar=float(CH) ** -0.5,
                                              in1=sqq[:, :], op0=ALU.mult, op1=ALU.mult), "kn")
                for d in range(2):
                    need(dve, "gcB", h, d + 1)
                    for c in range(NCH):
                        last = dve.tensor_scalar(DTm[:, d, c, :], PS[:, 6 + d, c * CH:(c + 1) * CH], hv[:, GC, c, d:d + 1], 0.0,
                                                 ALU.subtract, ALU.min)
                    told(last, "dmin")
                if not ends:
                    split_lo(dve, 0, u0 + h + 2)
                output_scaled(h)
                need(dve, "kT", h, 1)
                for d in range(2):
                    told(dve.tensor_tensor(kd[:, d, :, :], PS[:, 4, :].rearrange("p (c t) -> p c t", c=NCH),
                                           hv[:, EK, :, d:d + 1].to_broadcast([P, NCH, CH]), ALU.mult), "kd")
                need(dve, "gram", h, 1)
                for d in range(2):
                    need(dve, "mask", h, 3 * d + 3)
                    told(dve.tensor_tensor(NT[:, d, :, :], PS[:, 0, :].rearrange("p (c t) -> p c t", c=NCH), DTs[:, d, :, :], ALU.mult), "nt")
                for d in range(2):
                    need(dve, "nt", h, d + 1)
                    told(dve.tensor_tensor(BT[:, d, :, :], NT[:, d, :, :], const("bd16").unsqueeze(1).to_broadcast([P, NCH, CH]), ALU.mult), "b0")
                    need(dve, "nn", h, d + 1)
                    told(dve.tensor_tensor(BB[:, d, :, :], NN[:, d, :, :], const("bd16").unsqueeze(1).to_broadcast([P, NCH, CH]), ALU.mult), "b0")
                need(dve, "gram", h, 2)
                for d in range(2):
                    told(dve.tensor_tensor(at[:, d, :, :], PS[:, 2, 0:2 * CH].rearrange("p (c t) -> p c t", c=2), DTi[:, d, :, :], ALU.mult), "at")
                output_gated(h)
                ahead = [] if ends else list(conv_steps(h + 1))
                for rnd in range(10):
                    for d in range(2):
                        banks = ((1, 3, 6), (4, 5, 7))[d]
                        level = (rnd - 4) // 2
                        need(dve, "prod", h, 2 * rnd + d + 1)
                        if rnd == 0:
                            last = dve.tensor_copy(BB[:, d, :, :].rearrange("p c t -> p (c t)"), PS[:, banks[1], :])
                        elif rnd < 4:
                            xd = X[:, d, :, :].rearrange("p c t -> p (c t)")
                            last = dve.tensor_tensor(xd, xd, PS[:, banks[0], :], ALU.add)
                        elif rnd % 2 == 0:
                            last = dve.tensor_copy(BB[:, d, 0:2, :].rearrange("p c t -> p (c t)"), PS[:, banks[1], 0:256])
                        else:
                            xd = half_columns(X[:, d, :, :].rearrange("p c t -> p (c t)"), d, level)
                            last = dve.tensor_tensor(xd, xd, PS[:, banks[2], 0:256].rearrange("p (b j) -> p b j", j=16 << level), ALU.add)
                        told(last, "evd")
                        if ahead:
                            conv(h + 1, *ahead.pop(0))
                for j in range(NCH):
                    for d in range(2):
                        c = ORDER[d][j]
                        if j:
                            need(dve, "RS", h, 2 * (j - 1) + d + 1)
                            dve.scalar_tensor_tensor(out=r2[:, d, :], in0=PS[:, (1, 4)[d], 0:CH], scalar=hv[:, EG, c, d:d + 1],
                                                     in1=vt[:, c, :], op0=ALU.mult, op1=ALU.subtract).then_inc(gs_["r2"], 1)
                    for d in range(2):
                        c = ORDER[d][j]
                        need(dve, "TV", h, 2 * j + d + 1)
                        beta = hv[:, NBETA if j else BETA, c, d:d + 1]
                        told(dve.tensor_scalar(vn[:, d, :], PS[:, (3, 5)[d], 0:CH], beta, None, ALU.mult), "vn")
                    for d in range(2):
                        c = ORDER[d][j]
                        need(dve, "KV", h, 2 * j + d + 1)
                        if j == 0:
                            told(dve.tensor_copy(S[:, d, :], PS[:, (0, 2)[d], 0:CH]), "S")
                        elif j < NCH - 1:
                            told(dve.scalar_tensor_tensor(out=S[:, d, :], in0=S[:, d, :], scalar=etv[:, c, d:d + 1],
                                                          in1=PS[:, (0, 2)[d], 0:CH], op0=ALU.mult, op1=ALU.add), "S")
                        if c >= 2:
                            need(dve, "o1", h, 2 * (j - 2) + d + 1)
                            told(dve.tensor_tensor(oo[:, d, c - 2, :], o1[:, d, :], PS[:, (0, 2)[d], CH:2 * CH], ALU.add), "oo")
                need(dve, "oo", h, 4)
                told(dve.tensor_tensor(oo[:, 0, :, :], oo[:, 0, :, :], oo[:, 1, :, :], ALU.add), "osum")

            with dve.Fori(0, H - 1) as h:
                head(h, False)
            head(H - 1, True)
            output_scaled(H)
            output_gated(H)

            def update(i, s):
                for ab in range(2):
                    dve.wait_ge(blk_done[s], 1 + BASE["wo"] // 2 + i + 1)
                    add_to_x(dve, 1, 1, 2 * (2 * i + s) + ab, CTX, 2 * ab + s, "turned").then_inc(x_ready[ab], 1)

            blocks(dve, "wo", split_lo, update)

        def gdn_pool(pool):
            def times_one(dst, src):
                return pool.tensor_tensor(dst[:, :].rearrange("p (a t) -> p a t", a=2), src[:, :].rearrange("p (a t) -> p a t", a=2),
                                          const("one").unsqueeze(1).to_broadcast([P, 2, CH]), ALU.mult)

            def split_output(h):
                need(pool, "yt", h, 1)
                told(pool.tensor_copy(yh[:, bass.ds(h, 1), :], yt[:, :].unsqueeze(1)), "yh")
                need(pool, "yh", h, 1)
                told(pool.tensor_tensor(yl[:, bass.ds(h, 1), :], yt[:, :].unsqueeze(1), yh[:, bass.ds(h, 1), :].bitcast(F32), ALU.subtract), "yl")

            pool.wait_ge(gate_done, 1)
            pool.wait_ge(zg_zero, 1)
            with pool.Fori(0, H) as h:
                pool.wait_ge(gs_["yt"], 1 + h)
                told(times_one(zo, zg), "zo")
                need(pool, "zo", h, 1)
                need(pool, "zg", h, 1)
                told(times_one(zg, zn), "zc")
                for d in range(2):
                    need(pool, "dexp", h, d + 1)
                    tri = const(f"tri{d}").unsqueeze(1).to_broadcast([P, 2, CH])
                    strict = const(f"strict{d}").unsqueeze(1).to_broadcast([P, NCH, CH])
                    told(pool.tensor_tensor(DTi[:, d, :, :], DTm[:, d, 2:4, :], tri, ALU.mult), "mask")
                    told(pool.tensor_tensor(DTs[:, d, :, :], DTm[:, d, :, :], strict, ALU.mult), "mask")
                    need(pool, "mask", h, 3 * d + 2)
                    told(pool.tensor_tensor(DTs[:, d, :, :], DTs[:, d, :, :], hv[:, NBETA, :, d:d + 1].to_broadcast([P, NCH, CH]), ALU.mult),
                         "mask")
                for d in range(2):
                    need(pool, "b0", h, 2 * d + 1)
                    told(pool.tensor_tensor(X[:, d, :, :], BT[:, d, :, :], const("eye").unsqueeze(1).to_broadcast([P, NCH, CH]), ALU.add), "x0")
                for d in range(2):
                    need(pool, "nn", h, d + 1)
                    for n, name in enumerate(("e32", "e64", "e128")):
                        last = pool.tensor_tensor(EE[:, d, n, :, :], NN[:, d, :, :], const(name).unsqueeze(1).to_broadcast([P, NCH, CH]), ALU.mult)
                    told(last, "ee")
                split_output(h)
            pool.wait_ge(gs_["yt"], 1 + H)
            told(times_one(zo, zg), "zo")
            split_output(H)


        block = ctx.enter_context(nc.Block())

        def prime(eng, *sems):
            for group in sems:
                for one in group:
                    eng.sem_inc(one, 1)

        @block.sync
        def _(sp):
            def load_mods(i, slots=range(MS)):
                for s in slots:
                    sp.wait_ge(mod_used[s], 1 + i)
                    sp.dma_start(modw[:, s, :, :], A["mod_w"][bass.ds(MS * i + s, 1)].rearrange("a p k n -> (a p) k n")).then_inc(mod_in[s], 16)

            for dst, src in ((cvec[:, :, :], A["cvec"]), (consts[:, :, :], A["consts"])):
                sp.dma_start(dst, src).then_inc(c_in, 16)
            sp.dma_start(s5p[:, :, :], A["s5_a"]).then_inc(s5_par, 16)
            load_mods(0, range(1))
            for dst, src in ((sB[:, :, :, :], A["s5_b"]), (sC[:, :, :, :], A["s5_c"]), (sd[:, :], A["s5_d"]), (glub[:, :, :], A["glu_b"])):
                sp.dma_start(dst, src).then_inc(s5_par, 16)
            load_mods(0, range(1, MS))
            for dst, src in ((x[:, :, :], A["x"]), (ng[:, :, :, :], A["norm_g"]), (fg[:, :], A["final_g"]), (modb[:, :, :], A["mod_b"])):
                sp.dma_start(dst, src).then_inc(par_in, 16)
            with sp.Fori(1, MB // MS) as i:
                load_mods(i)
            for name, _, _ in PHASES:
                if name == "glu":
                    load_blocks(sp, name, 0, 1)
                    s5_sp(sp)
                    load_blocks(sp, name, 1)
                elif name == "gdn":
                    load_blocks(sp, name, 0, 1)
                    for s in range(2):
                        sp.wait_ge(x_ready[s], 1 + KT // 2 * 4)
                    for dst, src in ((gwa[:, :, :], A["g_w"]), (convw[:, :, :, :], A["g_conv"]), (gpar[:, :, :], A["g_par"]), (gng[:, :], A["g_ng"])):
                        sp.dma_start(dst, src).then_inc(gp_in, 16)
                    load_blocks(sp, name, 1)
                else:
                    load_blocks(sp, name)
            if "final" in STAGES:
                sp.wait_ge(fin_ready, KT)
                sp.dma_start(out, tmp[:, :, CTX:T]).then_inc(out_done, 16)
            else:
                for q in range(2):
                    sp.wait_ge(x_ready[q], 1 + KT // 2 * len(NORMS))
                sp.dma_start(out, x[:, :, :]).then_inc(out_done, 16)
            sp.wait_ge(out_done, 16)

        @block.scalar
        def _(act):
            act.wait_ge(c_in, 32)
            act.activation(cvec[:, :, :], cvec[:, :, :], ACT.Silu).then_inc(silu_c, 1)
            prep_act(act)
            split_hi(act, 0, 0)
            norm_act(act, 0)
            ffn_act(act, 0)
            if "s5" in STAGES:
                norm_act(act, 1)
                s5_act(act)
                norm_act(act, 2)
                ffn_act(act, 1)
            if "gdn" in STAGES:
                norm_act(act, 3)
                ffn_act(act, 2)
                norm_act(act, 4)
                gdn_act(act)
                norm_act(act, 5)
                ffn_act(act, 3)
            if "final" in STAGES:
                norm_act(act, 6)

        @block.tensor
        def _(pe):
            prime(pe, blk_done, mod_used, [mod_turned] * 2)
            prep_pe(pe)
            norm_pe(pe, 0)
            ffn_pe(pe, 0)
            if "s5" in STAGES:
                norm_pe(pe, 1)
                s5_pe(pe)
                glu_pe(pe)
                norm_pe(pe, 2)
                ffn_pe(pe, 1)
            if "gdn" in STAGES:
                norm_pe(pe, 3)
                ffn_pe(pe, 2)
                norm_pe(pe, 4)
                gdn_pe(pe)
                norm_pe(pe, 5)
                ffn_pe(pe, 3)
            if "final" in STAGES:
                norm_pe(pe, 6)

        @block.vector
        def _(dve):
            prime(dve, wlo_ready, gt_ready, x_ready, glu_ready, [gs_["yt"]])
            prep_dve(dve)
            mods_dve(dve)
            split_lo(dve, 0, 0)
            norm_dve(dve, 0)
            ffn_dve(dve, 0)
            if "s5" in STAGES:
                norm_dve(dve, 1)
                s5_dve(dve)
                norm_dve(dve, 2)
                ffn_dve(dve, 1)
            if "gdn" in STAGES:
                norm_dve(dve, 3)
                ffn_dve(dve, 2)
                norm_dve(dve, 4)
                gdn_dve(dve)
                norm_dve(dve, 5)
                ffn_dve(dve, 3)
            if "final" in STAGES:
                final_dve(dve)

        @block.gpsimd
        def _(pool):
            prime(pool, hid_ready, [gs_["yl"], gs_["zc"]])
            squares_pool(pool, 0)
            prep_pool(pool)
            ffn_pool(pool, 0)
            if "s5" in STAGES:
                squares_pool(pool, 1)
                s5_pool(pool)
                squares_pool(pool, 2)
                ffn_pool(pool, 1)
            if "gdn" in STAGES:
                squares_pool(pool, 3)
                ffn_pool(pool, 2)
                squares_pool(pool, 4)
                gdn_pool(pool)
                squares_pool(pool, 5)
                ffn_pool(pool, 3)
            if "final" in STAGES:
                squares_pool(pool, 6)


def constants():
    r, c = np.arange(P)[:, None], np.arange(P)[None, :]
    same = {b: r // b == c // b for b in (16, 32, 64, 128)}
    made = {"mean": np.full((P, P), 1.0 / D), "one": np.ones((P, P)), "eye": r == c,
            "tri0": r <= c, "tri1": r >= c, "strict0": r < c, "strict1": r > c, "bd16": same[16],
            "m16": r % C16 == c, "e32": same[32] & ~same[16], "e64": same[64] & ~same[32], "e128": same[128] & ~same[64]}
    return np.stack([np.asarray(made[n], np.float32) for n in CONSTS], axis=1)


def tiles(v):
    v = np.asarray(v)
    return np.moveaxis(v.reshape(*v.shape[:-1], KT, P), -1, 0)


def weight_blocks(w, cut):
    k, n = w.shape[0] // P, w.shape[1]
    t = w.reshape(k, P, n // P, P)
    return np.stack([t[:, :, c, :].transpose(1, 0, 2, 3).reshape(P, -1) for c in cut])


def layout_s5(I):
    def states(a):
        n = a.ndim
        a = a.reshape(2, PR, 2, 64, *a.shape[3:])
        return a.transpose(2, 3, 1, 0, *range(4, n + 1)).reshape(P, 64, *a.shape[4:])

    dt = np.broadcast_to(I["s5_log_dt"][0][:, :, None], (2, G, 64))
    b = np.stack([I["s5_b_re"][0], I["s5_b_im"][0]], axis=3)
    c = np.stack([I["s5_c_re"][0], I["s5_c_im"][0]], axis=3).transpose(0, 1, 4, 3, 2)
    return {"s5_a": np.stack([states(I["s5_a_re"][0]), states(I["s5_a_im"][0]), states(dt)], axis=1),
            "s5_b": states(b), "s5_c": states(c), "s5_d": tiles(I["s5_d"][0]),
            "glu_b": tiles(I["s5_glu_b"][0].reshape(2, D)),
            "w_glu": weight_blocks(I["s5_glu_w"][0], [[j, KT + j] for j in range(KT)])}


def layout_gdn(I):
    w = I["gdn_w_in"][0]
    conv = I["gdn_conv_w"][0].reshape(5, 3, H, P).transpose(3, 2, 1, 0)
    par = np.stack([I["gdn_a_log"][0].reshape(2 * H), I["gdn_dt_bias"][0].reshape(2 * H)])
    return {"w_gdn": weight_blocks(w[:, :4 * D], [c for h in range(H) for c in ([H + h, 2 * H + h], [h, 3 * H + h])]),
            "w_wo": weight_blocks(I["gdn_w_out"][0], [[2 * j, 2 * j + 1] for j in range(KT // 2)]),
            "g_w": w[:, 4 * D:].reshape(KT, P, 4 * H).transpose(1, 0, 2), "g_conv": conv,
            "g_par": np.broadcast_to(par, (P, 2, 2 * H)), "g_ng": I["gdn_norm_g"][0].reshape(P, 1)}


def layout(inputs):
    I = {n: np.asarray(v) for n, v in inputs.items()}
    a = {"x": np.ascontiguousarray(tiles(np.concatenate([I["ctx"][0], I["x"][0]], axis=0)).transpose(0, 2, 1)),
         "consts": constants(),
         "cvec": np.stack([tiles(I["c_ctx"]), tiles(I["c"][0])], axis=-1),
         "norm_g": tiles(I["norm_g"]), "final_g": tiles(I["final_g"]),
         "mod_b": I["mod_b"].reshape(2, NMOD * KT, P).transpose(2, 0, 1),
         "mod_w": I["mod_w"].reshape(2, KT, P, MB // 2, 256).transpose(0, 3, 2, 1, 4).reshape(MB, P, KT, 256)}
    for f in range(4):
        w13, w2 = I["ffn_w13"][f // 2, f % 2], I["ffn_w2"][f // 2, f % 2]
        if f"f{f}a" not in COUNT:
            continue
        a[f"w_f{f}a"] = weight_blocks(w13, [[j, FT + j] for j in range(FT)])
        t = w2.reshape(2, FH, P, KT, P)
        a[f"w_f{f}b"] = t.transpose(3, 0, 2, 1, 4).reshape(2 * KT, P, FH * P)
    a.update(layout_s5(I))
    if "gdn" in STAGES:
        a.update(layout_gdn(I))
    return {n: np.ascontiguousarray(v) for n, v in a.items()}


STAGES = ("s5", "gdn", "final")


def kernel(**inputs):
    from concourse import bacc
    from concourse.bass_utils import run_bass_kernel_spmd

    nc = bacc.Bacc("TRN2", target_bir_lowering=False, num_devices=1)
    arrays = layout(inputs)
    aps = {n: nc.dram_tensor("in_" + n, v.shape, F32, kind="ExternalInput").ap() for n, v in arrays.items()}
    out = nc.dram_tensor("out_0", (P, KT, LAT), F32, kind="ExternalOutput").ap()
    program(nc, aps, out)
    r = run_bass_kernel_spmd(nc, [{"in_" + n: v for n, v in arrays.items()}], core_ids=[0])
    y = r.results[0]["out_0"]
    return np.ascontiguousarray(y.transpose(2, 1, 0).reshape(1, LAT, D))
```
